# Optimizing a Trainium2 kernel written in Bass

```python
import math
import jax, jax.numpy as jnp
from jax import lax
import numpy as np

D_MODEL = 1024
BATCH = 1
SEQ = 512
DEPTH = 1

CHUNK = 64
N_META = 16
N_PAD = CHUNK - N_META
EPS = 1e-6

SSD_EXPAND = 2
SSD_D_INNER = SSD_EXPAND * D_MODEL
SSD_HEAD_DIM = 64
SSD_N_HEADS = SSD_D_INNER // SSD_HEAD_DIM
SSD_N_GROUPS = 8
SSD_HEADS_PER_GROUP = SSD_N_HEADS // SSD_N_GROUPS
SSD_D_STATE = 128
SSD_CONV_W = 4
SSD_CONV_DIM = SSD_D_INNER + 2 * SSD_N_GROUPS * SSD_D_STATE

SC_WIDTH = D_MODEL
SC_CONV_W = 3

N_BRANCH = 2

PEER_HEADS = 8
PEER_N_KEYS = 128
PEER_N_EXPERTS = PEER_N_KEYS * PEER_N_KEYS
PEER_D_KEY = 256
PEER_HALF = PEER_D_KEY // 2
PEER_TOPK = 16
PEER_BLOCK = CHUNK

PROJ_SIZES = (
    SSD_D_INNER,
    SSD_D_INNER,
    SSD_N_GROUPS * SSD_D_STATE,
    SSD_N_GROUPS * SSD_D_STATE,
    SSD_N_HEADS,
    SC_WIDTH,
    SC_WIDTH,
    SC_WIDTH,
    N_BRANCH * D_MODEL,
)
PROJ_TOTAL = sum(PROJ_SIZES)


def rmsnorm(x, g):
    xf = x.astype(jnp.float32)
    y = xf * lax.rsqrt(jnp.mean(xf * xf, axis=-1, keepdims=True) + EPS)
    return (y * g).astype(x.dtype)

def group_rmsnorm(y, g, groups):
    shp = y.shape
    yg = y.reshape(shp[:-1] + (groups, shp[-1] // groups)).astype(jnp.float32)
    yg = yg * lax.rsqrt(jnp.mean(yg * yg, axis=-1, keepdims=True) + EPS)
    return yg.reshape(shp) * g

def causal_dwconv(x, w):
    K = w.shape[-1]
    L = x.shape[1]
    xp = jnp.pad(x, ((0, 0), (K - 1, 0), (0, 0)))
    y = xp[:, 0:L, :] * w[:, 0]
    for k in range(1, K):
        y = y + xp[:, k:k + L, :] * w[:, k]
    return y

def ssd_chunked_scan(xdt, adt, bm, cm):
    b, L = xdt.shape[:2]
    nc = L // CHUNK

    def to_chunks(t):
        return jnp.moveaxis(t.reshape((b, nc, CHUNK) + t.shape[2:]), 1, 0)

    causal = jnp.tril(jnp.ones((CHUNK, CHUNK), dtype=bool))[None, :, :, None, None]

    def step(state, inp):
        xc, ac, bc, cc = inp
        acum = jnp.cumsum(ac.astype(jnp.float32), axis=1)
        seg = acum[:, :, None] - acum[:, None, :]
        decay = jnp.exp(jnp.where(causal, seg, -jnp.inf))
        cb = jnp.einsum('blgn,bsgn->blsg', cc, bc).astype(jnp.float32)
        y_diag = jnp.einsum('blsgr,bsgrp->blgrp', cb[..., None] * decay, xc)
        y_off = jnp.einsum('blgn,bgrpn->blgrp', cc, state) * jnp.exp(acum)[..., None]
        to_end = jnp.exp(acum[:, -1:] - acum)
        new_state = (state * jnp.exp(acum[:, -1])[..., None, None]
                     + jnp.einsum('blgn,blgr,blgrp->bgrpn', bc, to_end, xc))
        return new_state, y_diag + y_off

    state0 = jnp.zeros((b, SSD_N_GROUPS, SSD_HEADS_PER_GROUP, SSD_HEAD_DIM, SSD_D_STATE), jnp.float32)
    _, y = lax.scan(step, state0, (to_chunks(xdt), to_chunks(adt), to_chunks(bm), to_chunks(cm)))
    return jnp.moveaxis(y, 0, 1).reshape((b, L) + xdt.shape[2:])

def ssd_branch(z, xs, bs, cs, dt, valid, conv_w, conv_b, dt_bias, a_log, d_skip, norm_g, w_out):
    b, L, _ = xs.shape
    xbc = jnp.concatenate([xs, bs, cs], axis=-1)
    xbc = jax.nn.silu(causal_dwconv(xbc, conv_w) + conv_b) * valid
    xs = xbc[..., :SSD_D_INNER]
    bs = xbc[..., SSD_D_INNER:SSD_D_INNER + SSD_N_GROUPS * SSD_D_STATE]
    cs = xbc[..., SSD_D_INNER + SSD_N_GROUPS * SSD_D_STATE:]
    dt = jax.nn.softplus(dt.astype(jnp.float32) + dt_bias)
    a = -jnp.exp(a_log.astype(jnp.float32))
    xh = xs.reshape(b, L, SSD_N_GROUPS, SSD_HEADS_PER_GROUP, SSD_HEAD_DIM)
    dtg = dt.reshape(b, L, SSD_N_GROUPS, SSD_HEADS_PER_GROUP)
    y = ssd_chunked_scan(xh * dtg[..., None],
                         dtg * a.reshape(SSD_N_GROUPS, SSD_HEADS_PER_GROUP),
                         bs.reshape(b, L, SSD_N_GROUPS, SSD_D_STATE),
                         cs.reshape(b, L, SSD_N_GROUPS, SSD_D_STATE))
    y = y + xh * d_skip.reshape(SSD_N_GROUPS, SSD_HEADS_PER_GROUP)[..., None]
    y = y.reshape(b, L, SSD_D_INNER)
    y = group_rmsnorm(y * jax.nn.silu(z.astype(jnp.float32)), norm_g, SSD_N_GROUPS)
    return y.astype(xs.dtype) @ w_out

def shortconv_branch(sb, sc, sx, conv_w, w_out):
    return (sb * causal_dwconv(sc * sx, conv_w)) @ w_out

def peer_ffn(h, w_q, sub_keys, expert_u, expert_v):
    T, D = h.shape
    blocks = h.reshape(T // PEER_BLOCK, PEER_BLOCK, D)

    def one(xb):
        q = (xb @ w_q).reshape(PEER_BLOCK, PEER_HEADS, 2, PEER_HALF)
        s = jnp.einsum('thjd,hjkd->thjk', q, sub_keys).astype(jnp.float32)
        sv, si = lax.top_k(s, PEER_TOPK)
        cand = sv[:, :, 0, :, None] + sv[:, :, 1, None, :]
        cs, ci = lax.top_k(cand.reshape(PEER_BLOCK, PEER_HEADS, PEER_TOPK * PEER_TOPK), PEER_TOPK)
        i1 = jnp.take_along_axis(si[:, :, 0], ci // PEER_TOPK, axis=-1)
        i2 = jnp.take_along_axis(si[:, :, 1], ci % PEER_TOPK, axis=-1)
        eidx = i1 * PEER_N_KEYS + i2
        g = jax.nn.softmax(cs, axis=-1)
        u = expert_u[eidx]
        v = expert_v[eidx]
        act = jax.nn.gelu(jnp.einsum('td,thkd->thk', xb, u).astype(jnp.float32), approximate=False)
        return jnp.einsum('thk,thkd->td', (g * act).astype(v.dtype), v)

    return lax.map(one, blocks).reshape(T, D)

def first_inputs(seed: int = 0) -> dict:
    key = jax.random.key(seed)
    ks = jax.random.split(key, 22)
    f32 = jnp.float32

    def nrm(k, shape, scale):
        return jax.random.normal(k, shape, f32) * scale

    x = nrm(ks[0], (BATCH, SEQ, D_MODEL), 1.0)
    meta_tokens = nrm(ks[1], (N_META, D_MODEL), 1.0)
    ln_mix = 1.0 + nrm(ks[2], (DEPTH, D_MODEL), 0.02)
    w_in = nrm(ks[3], (DEPTH, D_MODEL, PROJ_TOTAL), D_MODEL ** -0.5)
    ssd_conv_w = nrm(ks[4], (DEPTH, SSD_CONV_DIM, SSD_CONV_W), SSD_CONV_W ** -0.5)
    ssd_conv_b = nrm(ks[5], (DEPTH, SSD_CONV_DIM), 0.01)
    dt0 = jnp.exp(jax.random.uniform(ks[6], (DEPTH, SSD_N_HEADS), f32, math.log(1e-3), math.log(1e-1)))
    ssd_dt_bias = dt0 + jnp.log(-jnp.expm1(-dt0))
    ssd_a_log = jnp.log(jax.random.uniform(ks[7], (DEPTH, SSD_N_HEADS), f32, 1.0, 16.0))
    ssd_d = 1.0 + nrm(ks[8], (DEPTH, SSD_N_HEADS), 0.02)
    ssd_norm = 1.0 + nrm(ks[9], (DEPTH, SSD_D_INNER), 0.02)
    ssd_w_out = nrm(ks[10], (DEPTH, SSD_D_INNER, D_MODEL), SSD_D_INNER ** -0.5)
    sc_conv_w = nrm(ks[11], (DEPTH, SC_WIDTH, SC_CONV_W), SC_CONV_W ** -0.5)
    sc_w_out = nrm(ks[12], (DEPTH, SC_WIDTH, D_MODEL), SC_WIDTH ** -0.5)
    w_o = nrm(ks[13], (DEPTH, D_MODEL, D_MODEL), D_MODEL ** -0.5)
    ln_ffn = 1.0 + nrm(ks[14], (DEPTH, D_MODEL), 0.02)
    peer_w_q = nrm(ks[15], (DEPTH, D_MODEL, PEER_HEADS * PEER_D_KEY), D_MODEL ** -0.5)
    peer_sub_keys = nrm(ks[16], (DEPTH, PEER_HEADS, 2, PEER_N_KEYS, PEER_HALF), PEER_HALF ** -0.5)
    peer_u = nrm(ks[17], (DEPTH, PEER_N_EXPERTS, D_MODEL), D_MODEL ** -0.5)
    peer_v = nrm(ks[18], (DEPTH, PEER_N_EXPERTS, D_MODEL), PEER_HEADS ** -0.5)
    ln_final = 1.0 + nrm(ks[19], (D_MODEL,), 0.02)
    return {"x": x, "meta_tokens": meta_tokens, "ln_mix": ln_mix, "w_in": w_in,
            "ssd_conv_w": ssd_conv_w, "ssd_conv_b": ssd_conv_b, "ssd_dt_bias": ssd_dt_bias,
            "ssd_a_log": ssd_a_log, "ssd_d": ssd_d, "ssd_norm": ssd_norm, "ssd_w_out": ssd_w_out,
            "sc_conv_w": sc_conv_w, "sc_w_out": sc_w_out, "w_o": w_o, "ln_ffn": ln_ffn,
            "peer_w_q": peer_w_q, "peer_sub_keys": peer_sub_keys, "peer_u": peer_u,
            "peer_v": peer_v, "ln_final": ln_final}

def first_block(x, meta_tokens, ln_mix, w_in, ssd_conv_w, ssd_conv_b, ssd_dt_bias, ssd_a_log, ssd_d,
              ssd_norm, ssd_w_out, sc_conv_w, sc_w_out, w_o, ln_ffn, peer_w_q, peer_sub_keys,
              peer_u, peer_v, ln_final):
    b = x.shape[0]
    pad = jnp.zeros((b, N_PAD, D_MODEL), x.dtype)
    meta = jnp.broadcast_to(meta_tokens[None].astype(x.dtype), (b, N_META, D_MODEL))
    h = jnp.concatenate([pad, meta, x], axis=1)
    lp = h.shape[1]
    valid = (jnp.arange(lp) >= N_PAD)[None, :, None].astype(x.dtype)
    split_idx = [int(c) for c in np.cumsum(PROJ_SIZES)[:-1]]

    for l in range(DEPTH):
        u = rmsnorm(h, ln_mix[l]) * valid
        proj = u @ w_in[l]
        z, xs, bs, cs, dt, sb, sc, sx, gates = jnp.split(proj, split_idx, axis=-1)
        y_ssd = ssd_branch(z, xs, bs, cs, dt, valid, ssd_conv_w[l], ssd_conv_b[l], ssd_dt_bias[l],
                           ssd_a_log[l], ssd_d[l], ssd_norm[l], ssd_w_out[l])
        y_sc = shortconv_branch(sb, sc, sx, sc_conv_w[l], sc_w_out[l])
        g = jax.nn.sigmoid(gates.astype(jnp.float32))
        merged = (g[..., :D_MODEL] * y_ssd + g[..., D_MODEL:] * y_sc).astype(x.dtype)
        h = h + merged @ w_o[l]
        u = rmsnorm(h, ln_ffn[l]) * valid
        ff = peer_ffn(u.reshape(-1, D_MODEL), peer_w_q[l], peer_sub_keys[l], peer_u[l], peer_v[l])
        h = h + ff.reshape(h.shape).astype(h.dtype)

    out = rmsnorm(h[:, N_PAD + N_META:], ln_final)
    return out


MIX_WIDTH = D_MODEL
ATTN_WIDTH = MIX_WIDTH // 2
N_HEADS = 8
HEAD_DIM = ATTN_WIDTH // N_HEADS
POOL_WIDTH = MIX_WIDTH - ATTN_WIDTH
POOL_WINDOWS = (2, 4, 8, 16)
N_POOL_GROUPS = len(POOL_WINDOWS)
POOL_GROUP = POOL_WIDTH // N_POOL_GROUPS
IN_WIDTH = 3 * ATTN_WIDTH + N_HEADS + POOL_WIDTH
D_FF = -(-(8 * D_MODEL) // (3 * 256)) * 256
Q_BLOCK = 128


def rmsnorm_2(x, g):
    xf = x.astype(jnp.float32)
    y = xf * lax.rsqrt(jnp.mean(xf * xf, axis=-1, keepdims=True) + EPS)
    return (y * g.astype(jnp.float32)).astype(x.dtype)

def forgetting_attention(q, k, v, log_f):
    S, Dh = q.shape[2], q.shape[3]
    c = jnp.cumsum(log_f, axis=-1)
    qf = q.astype(jnp.float32) * (Dh ** -0.5)
    kf = k.astype(jnp.float32)
    vf = v.astype(jnp.float32)
    outs = []
    for i in range(S // Q_BLOCK):
        q0, q1 = i * Q_BLOCK, (i + 1) * Q_BLOCK
        logits = jnp.einsum('bhqd,bhkd->bhqk', qf[:, :, q0:q1], kf[:, :, :q1])
        logits = logits + c[:, :, q0:q1, None] - c[:, :, None, :q1]
        t_pos = jnp.arange(q0, q1)[:, None]
        s_pos = jnp.arange(q1)[None, :]
        logits = jnp.where(s_pos <= t_pos, logits, -jnp.inf)
        p = jax.nn.softmax(logits, axis=-1)
        outs.append(jnp.einsum('bhqk,bhkd->bhqd', p, vf[:, :, :q1]))
    return jnp.concatenate(outs, axis=2).astype(q.dtype)

def multiscale_pool(u, w_pool, pool_scale):
    B, S, C = u.shape
    uf = u.astype(jnp.float32)
    cs = jnp.concatenate([jnp.zeros((B, 1, C), jnp.float32), jnp.cumsum(uf, axis=1)], axis=1)
    t = jnp.arange(S)
    groups = []
    for g, w in enumerate(POOL_WINDOWS):
        lo, hi = g * POOL_GROUP, (g + 1) * POOL_GROUP
        start = jnp.maximum(t + 1 - w, 0)
        csg = cs[:, :, lo:hi]
        window_sum = csg[:, 1:] - csg[:, start]
        count = (t + 1 - start).astype(jnp.float32)[None, :, None]
        groups.append(window_sum / count - uf[:, :, lo:hi])
    pooled = jnp.stack(groups, axis=2)
    mixed = jnp.einsum('bsgc,gcd->bsgd', pooled, w_pool.astype(jnp.float32)).reshape(B, S, C)
    return (mixed * pool_scale.astype(jnp.float32)).astype(u.dtype)

def second_inputs(seed: int = 0) -> dict:
    key = jax.random.key(seed)
    ks = jax.random.split(key, 13)
    f32 = jnp.float32
    nrm = lambda k, shape, scale: jax.random.normal(k, shape, f32) * scale
    return {
        "x": jax.random.normal(ks[0], (BATCH, SEQ, D_MODEL), f32),
        "norm1_g": 1.0 + nrm(ks[1], (DEPTH, D_MODEL), 0.05),
        "w_in": nrm(ks[2], (DEPTH, D_MODEL, IN_WIDTH), D_MODEL ** -0.5),
        "b_forget": 2.0 + nrm(ks[3], (DEPTH, N_HEADS), 0.5),
        "w_pool": nrm(ks[4], (DEPTH, N_POOL_GROUPS, POOL_GROUP, POOL_GROUP), POOL_GROUP ** -0.5),
        "pool_scale": 1.0 + nrm(ks[5], (DEPTH, POOL_WIDTH), 0.1),
        "w_out": nrm(ks[6], (DEPTH, MIX_WIDTH, D_MODEL), MIX_WIDTH ** -0.5),
        "norm2_g": 1.0 + nrm(ks[7], (DEPTH, D_MODEL), 0.05),
        "w_gate": nrm(ks[8], (DEPTH, D_MODEL, D_FF), D_MODEL ** -0.5),
        "w_up": nrm(ks[9], (DEPTH, D_MODEL, D_FF), D_MODEL ** -0.5),
        "w_down": nrm(ks[10], (DEPTH, D_FF, D_MODEL), D_FF ** -0.5),
        "final_g": 1.0 + nrm(ks[11], (D_MODEL,), 0.05),
    }

def second_block(x, norm1_g, w_in, b_forget, w_pool, pool_scale, w_out, norm2_g, w_gate, w_up, w_down, final_g):
    B, S, _ = x.shape
    for layer in range(DEPTH):
        h = rmsnorm_2(x, norm1_g[layer])
        proj = jnp.einsum('bsd,de->bse', h, w_in[layer])
        a0 = ATTN_WIDTH
        q = proj[..., 0:a0]
        k = proj[..., a0:2 * a0]
        v = proj[..., 2 * a0:3 * a0]
        f_logit = proj[..., 3 * a0:3 * a0 + N_HEADS]
        u = proj[..., 3 * a0 + N_HEADS:]
        to_heads = lambda t: t.reshape(B, S, N_HEADS, HEAD_DIM).transpose(0, 2, 1, 3)
        log_f = jax.nn.log_sigmoid(f_logit.astype(jnp.float32) + b_forget[layer].astype(jnp.float32))
        log_f = log_f.transpose(0, 2, 1)
        attn = forgetting_attention(to_heads(q), to_heads(k), to_heads(v), log_f)
        attn = attn.transpose(0, 2, 1, 3).reshape(B, S, ATTN_WIDTH)
        pool = multiscale_pool(u, w_pool[layer], pool_scale[layer])
        mixed = jnp.concatenate([attn, pool], axis=-1)
        x = x + jnp.einsum('bse,ed->bsd', mixed, w_out[layer])
        h2 = rmsnorm_2(x, norm2_g[layer])
        gate = jnp.einsum('bsd,df->bsf', h2, w_gate[layer])
        up = jnp.einsum('bsd,df->bsf', h2, w_up[layer])
        x = x + jnp.einsum('bsf,fd->bsd', jax.nn.silu(gate) * up, w_down[layer])
    return rmsnorm_2(x, final_g)


def setup_inputs(seed=0):
    out = dict(first_inputs(seed))
    for name, value in second_inputs(seed + 1).items():
        if name != "x":
            out[name + "_2"] = value
    return out


def reference(
    x, meta_tokens, ln_mix, w_in, ssd_conv_w, ssd_conv_b, ssd_dt_bias, ssd_a_log, ssd_d,
    ssd_norm, ssd_w_out, sc_conv_w, sc_w_out, w_o, ln_ffn, peer_w_q, peer_sub_keys, peer_u,
    peer_v, ln_final, norm1_g_2, w_in_2, b_forget_2, w_pool_2, pool_scale_2, w_out_2, norm2_g_2,
    w_gate_2, w_up_2, w_down_2, final_g_2,
):
    x = first_block(
        x, meta_tokens, ln_mix, w_in, ssd_conv_w, ssd_conv_b, ssd_dt_bias, ssd_a_log, ssd_d,
        ssd_norm, ssd_w_out, sc_conv_w, sc_w_out, w_o, ln_ffn, peer_w_q, peer_sub_keys, peer_u,
        peer_v, ln_final,
    )
    return second_block(
        x, norm1_g_2, w_in_2, b_forget_2, w_pool_2, pool_scale_2, w_out_2, norm2_g_2, w_gate_2,
        w_up_2, w_down_2, final_g_2,
    )


_drawn_inputs = setup_inputs


def setup_inputs(seed=0):
    import zlib

    import numpy as np

    out = dict(_drawn_inputs(seed))
    spreads = {}
    factors = {'ssd_conv_b': 3.663, 'ssd_d': 12.163, 'ssd_norm': 3.027, 'ln_ffn': 3.686}
    for name, (base, spread) in spreads.items():
        noise = np.random.default_rng([zlib.crc32(name.encode()), seed]).standard_normal(out[name].shape)
        drawn = base * np.exp(spread * noise) if base else spread * noise
        out[name] = __import__('jax').numpy.asarray(drawn.astype(out[name].dtype))
    for name, factor in factors.items():
        out[name] = (out[name] * factor).astype(out[name].dtype)
    return out
```

```python
from contextlib import ExitStack

import numpy as np
import concourse.bass as bass
from concourse import mybir

F32 = mybir.dt.float32
U32 = mybir.dt.uint32
ALU = mybir.AluOpType
ACT = mybir.ActivationFunctionType
AX = mybir.AxisListType
MUL, ADD, SUB = ALU.mult, ALU.add, ALU.subtract

T = 512
NT = 4
META = 16
L = META + T
HL = L // 2
G = 8
NEG = -3.0e38


class Queue:

    def __init__(self, sem, chain):
        self.sem, self.chain, self.n, self.items, self.seen = sem, chain, 0, [], {}

    def waits(self, after):
        need = {}

        def walk(x):
            if x is None:
                return
            if isinstance(x, tuple) and len(x) == 2 and isinstance(x[1], int):
                s, v = x
                if need.get(id(s), (s, 0))[1] < v:
                    need[id(s)] = (s, v)
            else:
                for y in x:
                    walk(y)

        walk(after)
        for k, (s, v) in need.items():
            if self.seen.get(k, 0) < v:
                self.seen[k] = v
                self.items.append(("wait", s, v))

    def __call__(self, fn, *after, mark=True):
        if self.chain and self.n:
            after = after + ((self.sem, self.n),)
        self.waits(after)
        if mark:
            self.n += 1
            self.items.append(("op", fn, self.sem, 1))
            return (self.sem, self.n)
        self.items.append(("op", fn, None, 0))
        return None

    def last(self):
        return (self.sem, self.n)

    def emit(self, eng):
        for it in self.items:
            if it[0] == "wait":
                eng.wait_ge(it[1], it[2])
            else:
                ins = it[1](eng)
                if it[2] is not None:
                    ins.then_inc(it[2], it[3])


class Lane:

    def __init__(self, sem):
        self.sem, self.n = sem, 0

    def start(self, queue, fn, *after):
        queue.waits((after, (self.sem, self.n) if self.n else None))
        self.n += 16
        queue.items.append(("op", fn, self.sem, 16))
        return (self.sem, self.n)


def b3(ap, n):
    return ap.unsqueeze(2).to_broadcast([ap.shape[0], ap.shape[1], n])


def bmid(ap, n):
    return ap.unsqueeze(1).to_broadcast([ap.shape[0], n, ap.shape[1]])


VEC = {}
_o = 0
for _k, _w in (("lnmix", 8), ("convw", 128), ("convb", 32), ("dskip", 16), ("normg", 16), ("scw", 24),
               ("dtb", 32), ("alog", 32), ("n1", 8), ("n2", 8), ("bf", 8), ("pscale", 4)):
    VEC[_k] = (_o, _o + _w)
    _o += _w
NVEC = _o
CON = {"ident": (0, 128), "ut": (128, 256), "sl": (256, 384), "neg": (384, 512), "ones": (512, 640),
       "iota": (640, 656), "rc": (656, 720)}
NCON = 720


def build(nc, A, out):
    with ExitStack() as ctx:
        sem = lambda n: ctx.enter_context(nc.semaphore(n))
        sbx = lambda cx, n, s, d=F32: cx.enter_context(nc.sbuf_tensor(n, s, d))
        sb = lambda n, s, d=F32: sbx(ctx, n, s, d)
        V, S, P, Gp, D = (Queue(sem("s_dve"), True), Queue(sem("s_act"), True), Queue(sem("s_pe"), False),
                          Queue(sem("s_pool"), True), Queue(sem("s_sp"), False))
        engines = (V, S, P, Gp)
        lane = lambda n: Lane(sem(n))

        con = sb("con", [128, NCON])
        vec = sb("vec", [128, NVEC])
        C = {k: con[:, a:b] for k, (a, b) in CON.items()}
        W = {k: vec[:, a:b] for k, (a, b) in VEC.items()}
        ident, ut, sl, neg, ones = C["ident"], C["ut"], C["sl"], C["neg"], C["ones"]
        h2 = sb("h2", [128, NT, 1024])
        wr = [sb(f"wr{i}", [128, 6144]) for i in range(2)]
        wlane = [lane(f"wl{i}") for i in range(2)]
        wfree = [None, None]
        wn = [0]
        sm = sb("sm", [128, 64])
        junk = sb("junk", [128, 1024])
        bank = [ctx.enter_context(nc.psum_tensor(f"ps{i}", [128, 512], F32)) for i in range(8)]
        bfree = [None] * 8
        bn = [0]

        def fence():
            return [q.last() for q in engines if q.n]

        def weights(src, n):
            i = wn[0] % 2
            wn[0] += 1
            tok = wlane[i].start(D, lambda e: e.dma_start(wr[i][:, 0:n], src), wfree[i])
            return i, wr[i], tok

        def take(n=1):
            if bn[0] % 8 + n > 8:
                bn[0] += 8 - bn[0] % 8
            i = bn[0] % 8
            bn[0] += n
            return i, [bfree[j] for j in range(i, i + n)]

        def mm(o, l, r, start, stop, *after, mark=False):
            return P(lambda e: e.matmul(o, l, r, start=start, stop=stop, skip_group_check=True), *after, mark=mark)

        def tr(o, i, idn, *after, mark=False):
            return P(lambda e: e.transpose(o, i, idn), *after, mark=mark)

        def vts(o, i, a, b, o0, o1=None, *after, q=V, **kw):
            return q(lambda e: e.tensor_scalar(o, i, a, b, o0, **({} if o1 is None else {"op1": o1}), **kw), *after)

        def vtt(o, a, b, op, *after, q=V):
            return q(lambda e: e.tensor_tensor(o, a, b, op), *after)

        def stt(o, a, s, b, op0, op1, *after):
            return V(lambda e: e.scalar_tensor_tensor(out=o, in0=a, scalar=s, in1=b, op0=op0, op1=op1), *after)

        def act(o, i, f, *after, **kw):
            return S(lambda e: e.activation(o, i, f, **kw), *after)

        def rsqrt(o, ss, tmp, inv_n, *after):
            v, a = tmp
            t = vts(v, ss, inv_n, 1e-6, MUL, ADD, *after)
            t = act(a, v, ACT.Ln, t)
            t = act(a, a, ACT.Exp, scale=-0.5)
            vtt(o, a, a, MUL, t)
            vtt(o, o, v, MUL)
            vts(o, o, -0.5, 1.5, MUL, ADD)
            return vtt(o, o, a, MUL)

        def softplus(o, x, tmp, *after):
            e, w, l = tmp
            vts(l, x, -1.0, None, MUL, None, *after)
            t = vtt(l, l, x, ALU.min)
            t = act(e, l, ACT.Exp, t)
            t = vts(w, e, 1.0, None, ADD, None, t)
            t = act(l, w, ACT.Ln, t)
            vts(w, w, -1.0, None, ADD, None, t)
            vts(o, w, 0.0, None, ALU.is_equal)
            vtt(l, l, o, ADD)
            vtt(w, w, o, ADD)
            V(lambda en: en.reciprocal(w, w))
            vtt(l, l, w, MUL)
            vtt(l, l, e, MUL)
            vts(o, x, 0.0, None, ALU.max)
            return vtt(o, o, l, ADD)

        def copy(o, i, *after):
            return V(lambda e: e.tensor_copy(o, i), *after)

        def mset(o, v, *after):
            return V(lambda e: e.memset(o, v), *after)

        def recip(o, i, *after):
            return V(lambda e: e.reciprocal(o, i), *after)

        def red(o, i, op, *after):
            return V(lambda e: e.tensor_reduce(o, i, AX.X, op), *after)

        def top8(v8, i8, x, drop, *after):
            V(lambda e: e.max(v8, x), *after)
            r = V(lambda e: e.max_index(i8, v8, x))
            if drop:
                r = V(lambda e: e.match_replace(out=x, in_to_replace=v8, in_values=x, imm_value=NEG))
            return r

        def store(ln, o, src, *after):
            return ln.start(D, lambda e: e.dma_start(o, src), *after)

        def load(name, o, src, *after):
            return lane(name).start(D, lambda e: e.dma_start(o, src), *after)

        t_con = load("l_con", con[:], A["con"])
        t_vec = load("l_vec", vec[:], A["vec"])
        x_src = A["x"].rearrange("(t p) d -> p t d", p=128)
        t_x = load("l_x", h2[:], x_src)

        with ExitStack() as pa:
            ab = lambda n, s, d=F32: sbx(pa, n, s, d)
            uT = ab("uT", [128, 8, L])
            ynT = ab("ynT", [128, 16, T])
            scT = ab("scT", [128, 8, T])
            with ExitStack() as pb:
                bb = lambda n, s, d=F32: sbx(pb, n, s, d)
                xm = bb("xm", [16, 1024])
                wdt = bb("wdt", [128, 256])
                xp = [bb(f"xp{i}", [128, 4, 3 + L]) for i in range(2)]
                xc = [bb(f"xc{i}", [128, 4, L]) for i in range(1)]
                zs = [bb(f"zs{i}", [128, 4, 256]) for i in range(2)]
                dD = bb("dD", [128, 2, 128])
                dt, av, ac, ea, te, et = [bb(n, [128, 5, 32]) for n in ("dt", "av", "ac", "ea", "te", "et")]
                sp = [bb(f"sp{i}", [128, 160]) for i in range(3)]
                aneg = bb("aneg", [128, 32])
                xdt = [bb(f"xdt{i}", [128, 256]) for i in range(2)]
                xw = [bb(f"xw{i}", [128, 256]) for i in range(2)]
                btm = [bb(f"btm{i}", [128, 128]) for i in range(2)]
                sla = [bb(f"sla{i}", [128, 4, 128]) for i in range(2)]
                mt = [bb(f"mt{i}", [128, 4, 128]) for i in range(2)]
                cbm = [bb(f"cbm{i}", [128, 128]) for i in range(2)]
                st = bb("st", [128, 256])
                y = bb("y", [128, 4, 256])
                ss = bb("ss", [128, 8])
                tmpx = bb("tmpx", [128, L])

                t_xm = load("l_xm", xm[:], A["meta"])
                t_wdt = load("l_wdt", wdt[:], A["wdt"])
                for t in range(NT):
                    tt = act(junk[:], h2[:, t, :], ACT.Square, t_x, accum_out=sm[:, t:t + 1])
                tz = mset(sm[:, 4:5], 1.0)
                tt = act(junk[0:16, :], xm[:], ACT.Square, t_xm, tz, accum_out=sm[0:16, 4:5])
                r = rsqrt(sm[:, 8:13], sm[:, 0:5], (sm[:, 16:21], sm[:, 24:29]), 1.0 / 1024, tt)
                for t in range(5):
                    src = h2[:, t, :] if t < 4 else xm[:]
                    n = 128 if t < 4 else 16
                    col = META + 128 * t if t < 4 else 0
                    tk = vts(junk[0:n, :], src, sm[0:n, 8 + t:9 + t], None, MUL, None, P.last() if t else None)
                    i, fr = take(2)
                    for k in range(8):
                        ps = bank[i + k // 4]
                        m = tr(ps[:, (k % 4) * 128:(k % 4) * 128 + n], junk[0:n, k * 128:(k + 1) * 128],
                               ident[0:n, 0:n], fr, tk, t_con, mark=(k == 7))
                    for k in range(8):
                        ps = bank[i + k // 4]
                        tu = act(uT[:, k, col:col + n], ps[:, (k % 4) * 128:(k % 4) * 128 + n], ACT.Copy, m, t_vec,
                                 scale=W["lnmix"][:, k:k + 1])
                    bfree[i] = bfree[i + 1] = tu
                ta = act(aneg[:], W["alog"], ACT.Exp, t_vec)
                ta = vts(aneg[:], aneg[:], -1.0, None, MUL, None, ta)
                i, fr = take()
                mset(dt[:], 0.0)
                for c in range(5):
                    n, col = (16, 0) if c == 0 else (128, META + 128 * (c - 1))
                    for k in range(8):
                        m = mm(bank[i][0:n, 32 * c:32 * c + 32], uT[:, k, col:col + n], wdt[:, 32 * k:32 * k + 32],
                               k == 0, k == 7, tu, fr, t_wdt, mark=(k == 7))
                for c in range(5):
                    n = 16 if c == 0 else 128
                    td = vtt(dt[0:n, c, :], bank[i][0:n, 32 * c:32 * c + 32], W["dtb"][0:n, :], ADD, m)
                bfree[i] = td
                dflat, aflat = dt[:].rearrange("p c h -> p (c h)"), av[:].rearrange("p c h -> p (c h)")
                softplus(aflat, dflat, [x[:] for x in sp])
                copy(dflat, aflat)
                ta = vtt(av[:], dt[:], bmid(aneg[:], 5), MUL, q=V)
                i, fr = take(2)
                for c in range(5):
                    n = 16 if c == 0 else 128
                    mm(bank[i][0:n, 32 * c:32 * c + 32], ut[0:n, 0:n], av[0:n, c, :], True, True, ta, fr)
                    m = mm(bank[i + 1][:, 32 * c:32 * c + 32], ones[0:n, :], av[0:n, c, :], True, True, mark=True)
                mset(te[:], 0.0)
                for c in range(5):
                    n = 16 if c == 0 else 128
                    copy(ac[0:n, c, :], bank[i][0:n, 32 * c:32 * c + 32], m)
                    t1 = vtt(te[0:n, c, :], bank[i + 1][0:n, 32 * c:32 * c + 32], ac[0:n, c, :], SUB)
                for c in range(5):
                    n = 16 if c == 0 else 128
                    act(ea[0:n, c, :], ac[0:n, c, :], ACT.Exp, t1)
                    act(te[0:n, c, :], te[0:n, c, :], ACT.Exp)
                    t2 = act(et[:, c, :], bank[i + 1][:, 32 * c:32 * c + 32], ACT.Exp)
                bfree[i] = bfree[i + 1] = [t1, t2]
                t_dec = t2
                for b in range(2):
                    mset(xp[b][:, :, 0:3], 0.0)

                for j in range(8):
                    wi, w, tw = weights(A["wsc"][j], 3072)
                    bufs = []
                    for s_ in (2, 1, 0):
                        i, fr = take(2)
                        for hh in range(2):
                            for k in range(8):
                                m = mm(bank[i + hh][:, 0:HL], w[:, k * 384 + s_ * 128:k * 384 + s_ * 128 + 128],
                                       uT[:, k, hh * HL:(hh + 1) * HL], k == 0, k == 7, fr, tw, tu, mark=(k == 7))
                        bufs.append((i, m))
                    wfree[wi] = P.last()
                    (ix, mx), (ic, mc), (ib, mb) = bufs
                    pb_ = xp[j % 2]
                    dst, cv = pb_[:, 0, 1:3 + L], pb_[:, 1, 0:T]
                    for hh in range(2):
                        t1 = act(pb_[:, 2, hh * HL:(hh + 1) * HL], bank[ix + hh][:, 0:HL], ACT.Copy, mx, V.last())
                        bfree[ix + hh] = t1
                    for hh in range(2):
                        bfree[ic + hh] = vtt(pb_[:, 0, 3 + hh * HL:3 + (hh + 1) * HL], bank[ic + hh][:, 0:HL],
                                             pb_[:, 2, hh * HL:(hh + 1) * HL], MUL, t1, mc)
                    sw = W["scw"]
                    vts(cv, pb_[:, 0, 1 + META:1 + META + T], sw[:, 3 * j:3 * j + 1], None, MUL)
                    for k in (1, 2):
                        stt(cv, pb_[:, 0, 1 + META + k:1 + META + k + T], sw[:, 3 * j + k:3 * j + k + 1], cv, MUL, ADD)
                    a = HL - META
                    bfree[ib] = vtt(scT[:, j, 0:a], bank[ib][:, META:HL], cv[:, 0:a], MUL, mb)
                    t_sc = bfree[ib + 1] = vtt(scT[:, j, a:T], bank[ib + 1][:, 0:HL], cv[:, a:T], MUL)

                for g in range(G):
                    wi, w, tw = weights(A["wg"][g], 6144)
                    xq, xcg, zg = xp[g % 2], xc[0], zs[g % 2]
                    v_before = V.last()
                    for s_ in range(4):
                        i, fr = take(2)
                        for hh in range(2):
                            for k in range(8):
                                m = mm(bank[i + hh][:, 0:HL], w[:, k * 768 + s_ * 128:k * 768 + s_ * 128 + 128],
                                       uT[:, k, hh * HL:(hh + 1) * HL], k == 0, k == 7, fr, tw, mark=(k == 7))
                            bfree[i + hh] = te_ = act(xq[:, s_, 3 + hh * HL:3 + (hh + 1) * HL], bank[i + hh][:, 0:HL],
                                                      ACT.Copy, m, v_before)
                        if s_ == 0:
                            t0 = te_
                        cw, cvx = W["convw"], xcg[:, s_, :]
                        q4 = (4 * g + s_) * 4
                        vts(tmpx[:], xq[:, s_, 0:L], cw[:, q4:q4 + 1], None, MUL, None, te_)
                        for k in range(1, 4):
                            tv = stt(tmpx[:] if k < 3 else cvx, xq[:, s_, k:k + L], cw[:, q4 + k:q4 + k + 1],
                                     tmpx[:], MUL, ADD, P.last() if k == 3 else None)
                        t_xc = act(cvx, cvx, ACT.Silu, tv, bias=W["convb"][:, 4 * g + s_:4 * g + s_ + 1])
                    i, fr = take(2)
                    for c in range(4):
                        ps = bank[i + c // 2][:, (c % 2) * 256:(c % 2) * 256 + 256]
                        for k in range(8):
                            m = mm(ps, uT[:, k, META + 128 * c:META + 128 * c + 128],
                                   w[:, k * 768 + 512:k * 768 + 768], k == 0, k == 7, fr, tw, mark=(k == 7))
                    wfree[wi] = P.last()
                    for b in range(2):
                        bfree[i + b] = t_z = act(zg[:, 2 * b:2 * b + 2, :].rearrange("p a b -> p (a b)"),
                                                 bank[i + b][:], ACT.Silu, m, v_before)
                    for j in range(2):
                        t_dD = vts(dD[:, j, :], ident, W["dskip"][:, 2 * g + j:2 * g + j + 1], None, MUL, None, P.last())
                    for c in range(5):
                        n, col = (16, 0) if c == 0 else (128, META + 128 * (c - 1))
                        b = c % 2
                        i, fr = take()
                        for s_ in range(3):
                            m = tr(bank[i][0:n, s_ * 128:s_ * 128 + 128], xcg[:, s_, col:col + n], ident, fr, t_xc,
                                   mark=(s_ == 2))
                        tx = vtt(xdt[b][0:n, :].rearrange("p (h e) -> p h e", h=4),
                                 bank[i][0:n, 0:256].rearrange("p (h e) -> p h e", h=4),
                                 b3(dt[0:n, c, 4 * g:4 * g + 4], 64), MUL, m, P.last(), Gp.last())
                        tb = act(btm[b][0:n, :], bank[i][0:n, 256:384], ACT.Copy, tx)
                        bfree[i] = [tx, tb]
                        txw = vtt(xw[b][0:n, :].rearrange("p (h e) -> p h e", h=4),
                                  xdt[b][0:n, :].rearrange("p (h e) -> p h e", h=4),
                                  b3(te[0:n, c, 4 * g:4 * g + 4], 64), MUL, tx, t_dec, P.last(), q=Gp)
                        if c > 0:
                            tsl = vtt(sla[b][:], bmid(sl, 4), b3(av[:, c, 4 * g:4 * g + 4], 128), MUL, ta, P.last(),
                                      q=Gp)
                            i, fr = take()
                            for h in range(4):
                                m = mm(bank[i][:, 128 * h:128 * h + 128], sla[b][:, h, :], ut, h == 0, True, fr, tsl,
                                       mark=(h == 3))
                            tm = act(mt[b][:].rearrange("p a b -> p (a b)"), bank[i][:], ACT.Exp, m, V.last())
                            bfree[i] = tm
                            i, fr = take()
                            m = mm(bank[i][:, 0:128], xcg[:, 2, col:col + n], xcg[:, 3, col:col + n], True, True, fr,
                                   mark=True)
                            bfree[i] = vtt(cbm[b][:], bank[i][:, 0:128], ut, MUL, m)
                            tm = vtt(mt[b][:], mt[b][:], bmid(cbm[b][:], 4), MUL, tm)
                            i, fr = take()
                            yd, yo = bank[i][:, 0:256], bank[i][:, 256:512]
                            for j in range(2):
                                mm(bank[i][:, 128 * j:128 * j + 128], xcg[:, j, col:col + n], dD[:, j, :], j == 0,
                                   False, fr, t_dD)
                            for h in range(4):
                                mm(bank[i][:, 64 * h:64 * h + 64], mt[b][:, h, :], xdt[b][:, 64 * h:64 * h + 64],
                                   False, False, tm, tx)
                            m = mm(yo, xcg[:, 3, col:col + n], st[:], False, True, t_st, mark=True)
                            yc = y[:, c - 1, :]
                            vtt(yc.rearrange("p (h e) -> p h e", h=4), yo.rearrange("p (h e) -> p h e", h=4),
                                b3(ea[:, c, 4 * g:4 * g + 4], 64), MUL, m, t_dec, P.last(), S.last())
                            bfree[i] = vtt(yc, yc, yd, ADD)
                            ty = vtt(yc, yc, zg[:, c - 1, :], MUL, t_z)
                            tq = act(junk[:, 0:256], yc, ACT.Square, ty, accum_out=ss[:, c - 1:c])
                        if c < 4:
                            i, fr = take()
                            m = mm(bank[i][:, 0:256], btm[b][0:n, :], xw[b][0:n, :], True, True, fr, txw, tb, mark=True)
                            if c == 0:
                                t_st = copy(st[:], bank[i][:, 0:256], m, P.last())
                            else:
                                vtt(st[:].rearrange("p (h e) -> p h e", h=4),
                                    st[:].rearrange("p (h e) -> p h e", h=4),
                                    b3(et[:, c, 4 * g:4 * g + 4], 64), MUL, m, P.last())
                                t_st = vtt(st[:], st[:], bank[i][:, 0:256], ADD)
                            bfree[i] = t_st
                    r = rsqrt(sm[:, 8:12], ss[:, 0:4], (sm[:, 16:20], sm[:, 24:28]), 1.0 / 256, tq)
                    t_y = vtt(y[:], y[:], b3(sm[:, 8:12], 256), MUL)
                    for j in range(2):
                        i, fr = take()
                        for c in range(4):
                            m = tr(bank[i][:, 128 * c:128 * c + 128], y[:, c, 128 * j:128 * j + 128], ident, fr, t_y,
                                   mark=(c == 3))
                        bfree[i] = t_yn = act(ynT[:, 2 * g + j, :], bank[i][:], ACT.Copy, m,
                                              scale=W["normg"][:, 2 * g + j:2 * g + j + 1])
                f = fence()
            mg = ab("mg", [128, 8, T])
            g1 = ab("g1", [128, 2, T])
            xr = ab("xr", [128, NT, 1024])
            for j in range(8):
                wi, w, tw = weights(A["wgo"][j], 5120)
                ps = []
                for q_, (n, rhs) in enumerate(((8, uT), (8, uT), (16, ynT), (8, scT))):
                    base = (0, 1024, 2048, 4096)[q_]
                    i, fr = take()
                    off = META if q_ < 2 else 0
                    for k in range(n):
                        m = mm(bank[i][:], w[:, base + k * 128:base + k * 128 + 128], rhs[:, k, off:off + T],
                               k == 0, k == n - 1, fr, tw, t_yn, t_sc, f if j == 0 else None, mark=(k == n - 1))
                    ps.append((i, m))
                wfree[wi] = P.last()
                for q_ in range(2):
                    i, m = ps[q_]
                    bfree[i] = tg = act(g1[:, q_, :], bank[i][:], ACT.Sigmoid, m, V.last())
                i, m = ps[2]
                bfree[i] = vtt(g1[:, 0, :], g1[:, 0, :], bank[i][:], MUL, m, tg)
                i, m = ps[3]
                bfree[i] = vtt(g1[:, 1, :], g1[:, 1, :], bank[i][:], MUL, m)
                t_mg = vtt(mg[:, j, :], g1[:, 0, :], g1[:, 1, :], ADD)
            for hf in range(2):
                wi, w, tw = weights(A["wo"][hf], 4096)
                for t in range(NT):
                    i, fr = take()
                    for k in range(8):
                        m = mm(bank[i][:], mg[:, k, 128 * t:128 * t + 128], w[:, 512 * k:512 * k + 512],
                               k == 0, k == 7, fr, tw, t_mg, mark=(k == 7))
                    hs = h2[:, t, 512 * hf:512 * hf + 512]
                    bfree[i] = t_h2 = vtt(hs, hs, bank[i][:], ADD, m)
                wfree[wi] = P.last()
            f = fence()

        with ExitStack() as pa:
            ab = lambda n, s, d=F32: sbx(pa, n, s, d)
            u2 = ab("u2", [128, NT, 1024])
            row = ab("row", [128, 1024])
            eidx = ab("eidx", [128, NT, 128], U32)
            gate = ab("gate", [128, NT, 128])
            NR = 12
            ring = [ab(f"ring{i}", [128, 1024]) for i in range(NR)]
            t_row = load("l_row", row[:], A["lnffn"], f)
            with ExitStack() as pb:
                bb = lambda n, s, d=F32: sbx(pb, n, s, d)
                u2T = bb("u2T", [128, 8, T])
                keys = bb("keys", [128, 2048])
                q_sb = [bb(f"q_sb{i}", [128, T]) for i in range(2)]
                s_sb = [bb(f"s_sb{i}", [128, 512]) for i in range(2)]
                sv = bb("sv", [128, NT, 16, 16])
                si = bb("si", [128, NT, 16, 16], U32)
                sif = bb("sif", [128, 16, 16])
                cand = bb("cand", [128, 8, 256])
                cv = bb("cv", [128, 8, 16])
                ci = bb("ci", [128, 8, 16], U32)
                cx = [bb(f"cx{i}", [128, 8, 16]) for i in range(3)]
                cu = bb("cu", [128, 8, 16], U32)
                rd = bb("rd", [128, 8])
                t_keys = load("l_keys", keys[:], A["keys"], f)
                for t in range(NT):
                    tt = act(junk[:], h2[:, t, :], ACT.Square, f, accum_out=sm[:, t:t + 1])
                rsqrt(sm[:, 8:12], sm[:, 0:4], (sm[:, 16:20], sm[:, 24:28]), 1.0 / 1024, tt)
                for t in range(NT):
                    tk = stt(u2[:, t, :], h2[:, t, :], sm[:, 8 + t:9 + t], row[:], MUL, MUL, t_row)
                    i, fr = take(2)
                    for k in range(8):
                        ps = bank[i + k // 4]
                        m = tr(ps[:, (k % 4) * 128:(k % 4) * 128 + 128], u2[:, t, k * 128:(k + 1) * 128], ident,
                               fr, tk, mark=(k == 7))
                    for b in range(2):
                        tu = act(u2T[:, 4 * b:4 * b + 4, 128 * t:128 * t + 128],
                                 bank[i + b][:].rearrange("p (k e) -> p k e", k=4), ACT.Copy, m)
                        bfree[i + b] = tu
                for hj in range(16):
                    if hj % 4 == 0:
                        wi, w, tw = weights(A["wq"][hj // 4], 4096)
                    i, fr = take()
                    for k in range(8):
                        c0 = (hj % 4) * 1024 + k * 128
                        m = mm(bank[i][:], w[:, c0:c0 + 128], u2T[:, k, :], k == 0, k == 7, fr, tw, tu, mark=(k == 7))
                    if hj % 4 == 3:
                        wfree[wi] = P.last()
                    qq, s2 = q_sb[hj % 2], s_sb[hj % 2]
                    bfree[i] = tq = act(qq[:], bank[i][:], ACT.Copy, m, P.last())
                    i, fr = take()
                    for t in range(NT):
                        m = mm(bank[i][:, 128 * t:128 * t + 128], qq[:, 128 * t:128 * t + 128],
                               keys[:, 128 * hj:128 * hj + 128], t == 0, True, fr, tq, t_keys, mark=(t == 3))
                    bfree[i] = tsb = act(s2[:], bank[i][:], ACT.Copy, m, V.last())
                    for t in range(NT):
                        sx = s2[:, 128 * t:128 * t + 128]
                        for r_ in range(2):
                            top8(sv[:, t, hj, 8 * r_:8 * r_ + 8], si[:, t, hj, 8 * r_:8 * r_ + 8], sx, r_ == 0, tsb)
                t_e = []
                for t in range(NT):
                    copy(sif[:], si[:, t])
                    s4 = sv[:, t].rearrange("p (h j) k -> p h j k", j=2)
                    i4 = sif[:].rearrange("p (h j) k -> p h j k", j=2)
                    for h in range(8):
                        cd = cand[:, h, :].rearrange("p (a b) -> p a b", a=16)
                        vtt(cd, b3(s4[:, h, 0, :], 16), bmid(s4[:, h, 1, :], 16), ADD)
                        for r_ in range(2):
                            top8(cv[:, h, 8 * r_:8 * r_ + 8], ci[:, h, 8 * r_:8 * r_ + 8], cand[:, h, :], r_ == 0)
                    red(rd[:], cv[:], ALU.max)
                    gt = gate[:, t, :].rearrange("p (h k) -> p h k", h=8)
                    tg = vtt(gt, cv[:], b3(rd[:], 16), SUB)
                    tg = act(gate[:, t, :], gate[:, t, :], ACT.Exp, tg)
                    red(rd[:], gt, ADD, tg)
                    recip(rd[:], rd[:])
                    vtt(gt, gt, b3(rd[:], 16), MUL)
                    vts(cu[:], ci[:], 4, None, ALU.logical_shift_right)
                    copy(cx[0][:], cu[:])
                    vts(cu[:], ci[:], 15, None, ALU.bitwise_and)
                    copy(cx[1][:], cu[:])
                    for half in range(2):
                        for h in range(8):
                            oh = cand[:, h, :].rearrange("p (a b) -> p a b", a=16)
                            vtt(oh, b3(cx[half][:, h, :], 16), bmid(C["iota"], 16), ALU.is_equal)
                            vtt(oh, oh, bmid(i4[:, h, half, :], 16), MUL)
                        o = cx[half][:].rearrange("p h k -> p (h k)")
                        red(o, cand[:].rearrange("p h (a b) -> p (h a) b", b=16), ADD)
                    stt(cx[2][:], cx[0][:], 128.0, cx[1][:], MUL, ADD)
                    t_e.append(copy(eidx[:, t, :], cx[2][:].rearrange("p h k -> p (h k)")))
                f = fence()
            dots = ab("dots", [128, 128])
            wgt = ab("wgt", [128, 128])
            acc = ab("acc", [128, 1024])
            rl = [lane(f"rl{i}") for i in range(NR)]
            rf = [None] * NR
            rn = 0
            t_row = load("l_row2", row[:], A["lnfin"], f)

            def dot(a, b, o, *after):
                return V(lambda e: e.tensor_tensor_reduce(junk[:], a, b, 1.0, 0.0, MUL, ADD, o), *after)

            def gather(src, t, k):
                nonlocal rn
                s_ = rn % NR
                rn += 1
                tok = rl[s_].start(Gp, lambda e: e.indirect_dma_start(
                    ring[s_][:], None, src, bass.IndirectOffsetOnAxis(ap=eidx[:, t, k:k + 1], axis=0)),
                    t_e[t], rf[s_], f)
                return s_, tok

            AH = NR - 1
            jobs = [(src, t, k) for t in range(NT) for src in ("pu", "pv") for k in range(128)]
            got = [gather(A[jobs[n][0]], *jobs[n][1:]) for n in range(AH)]
            for n, (src, t, k) in enumerate(jobs):
                s_, tok = got[n]
                if src == "pu":
                    x = dot(ring[s_][:], u2[:, t, :], dots[:, k:k + 1], tok, f)
                else:
                    if k == 0:
                        ta = act(wgt[:], dots[:], ACT.Gelu, V.last())
                        vtt(wgt[:], wgt[:], gate[:, t, :], MUL, ta)
                    if k == 0:
                        x = vts(acc[:], ring[s_][:], wgt[:, 0:1], None, MUL, None, tok)
                    else:
                        x = stt(acc[:], ring[s_][:], wgt[:, k:k + 1], acc[:], MUL, ADD, tok)
                rf[s_] = x
                if n + AH < len(jobs):
                    got.append(gather(A[jobs[n + AH][0]], *jobs[n + AH][1:]))
                if src == "pv" and k == 127:
                    th = vtt(h2[:, t, :], h2[:, t, :], acc[:], ADD)
                    tt = act(u2[:, t, :], h2[:, t, :], ACT.Square, th, accum_out=sm[:, t:t + 1])
                    rsqrt(sm[:, 8:9], sm[:, t:t + 1], (sm[:, 16:17], sm[:, 24:25]), 1.0 / 1024, tt)
                    stt(h2[:, t, :], h2[:, t, :], sm[:, 8:9], row[:], MUL, MUL, t_row)
            f = fence()

        def turned(dst, gvec, *after):
            for t in range(NT):
                tt = act(junk[:], h2[:, t, :], ACT.Square, after, P.last(), V.last(), accum_out=sm[:, t:t + 1])
            rsqrt(sm[:, 8:12], sm[:, 0:4], (sm[:, 16:20], sm[:, 24:28]), 1.0 / 1024, tt)
            for t in range(NT):
                tk = vts(junk[:], h2[:, t, :], sm[:, 8 + t:9 + t], None, MUL, None, P.last())
                i, fr = take(2)
                for k in range(8):
                    ps = bank[i + k // 4]
                    m = tr(ps[:, (k % 4) * 128:(k % 4) * 128 + 128], junk[:, k * 128:(k + 1) * 128], ident,
                           fr, tk, mark=(k == 7))
                for k in range(8):
                    ps = bank[i + k // 4]
                    tu = act(dst[:, k, 128 * t:128 * t + 128], ps[:, (k % 4) * 128:(k % 4) * 128 + 128], ACT.Copy, m,
                             scale=gvec[:, k:k + 1])
                bfree[i] = bfree[i + 1] = tu
            return tu

        with ExitStack() as pa:
            ab = lambda n, s, d=F32: sbx(pa, n, s, d)
            hT = ab("hT", [128, 8, T])
            qk = ab("qk", [128, 8, T])
            mx = ab("mx", [128, 8, T])
            vt = ab("vt", [128, NT, 512])
            lf = ab("lf", [128, NT, 8])
            cq = ab("cq", [128, NT, 8])
            sp = [ab(f"sq{i}", [128, 32]) for i in range(3)]
            xx = ab("xx", [128, 32])
            cb = [ab(f"cb{i}", [128, T]) for i in range(8)]
            lg = [ab(f"lg{i}", [128, T]) for i in range(2)]
            pT = [ab(f"pT{i}", [128, T]) for i in range(2)]
            up = ab("up", [128, 16 + T])
            wsm = ab("wsm", [128, 64])
            wpl = ab("wpl", [128, 512])
            mxx = ab("mxx", [128, 16])
            den = ab("den", [128, 8])
            ao = ab("ao", [128, 512])
            t_ws = load("l_ws", wsm[:], A["wf2"], f)
            t_wp = load("l_wp", wpl[:], A["wpool"], f)
            tu = turned(hT, W["n1"], f)
            for s3 in range(3):
                wi, w, tw = weights(A["wqku"][s3], 4096)
                for s_ in range(4):
                    i, fr = take()
                    for k in range(8):
                        m = mm(bank[i][:], w[:, s_ * 1024 + k * 128:s_ * 1024 + k * 128 + 128], hT[:, k, :],
                               k == 0, k == 7, fr, tw, tu, mark=(k == 7))
                    if s3 < 2:
                        bfree[i] = t_qk = act(qk[:, 4 * s3 + s_, :], bank[i][:], ACT.Copy, m,
                                              scale=0.125 if s3 == 0 else 1.0)
                        continue
                    mset(up[:, 0:16], 0.0, P.last() if s_ == 0 else None)
                    x = copy(up[:, 16:16 + T], bank[i][:], m, P.last())
                    cur, other = junk[:, 0:T], junk[:, 512:1024]
                    d = 1
                    src = up
                    seq = [up[:, 0:16 + T]]
                    bufs = [lg[0], lg[1]]
                    prev_main, prev_head = up[:, 16:16 + T], None
                    for lv in range(s_ + 1):
                        o = bufs[lv % 2]
                        vtt(o[:, d:T], prev_main[:, d:T], prev_main[:, 0:T - d], ADD)
                        copy(o[:, 0:d], prev_main[:, 0:d])
                        prev_main = o[:, 0:T]
                        d *= 2
                    wd = 2 << s_
                    pl = bufs[(s_ + 1) % 2]
                    hd = C["rc"][:, 16 * s_:16 * s_ + 16]
                    vtt(pl[:, 0:16], prev_main[:, 0:16], hd, MUL)
                    vts(pl[:, 16:T], prev_main[:, 16:T], 1.0 / wd, None, MUL)
                    tp = vtt(up[:, 16:16 + T], pl[:], up[:, 16:16 + T], SUB)
                    bfree[i] = x
                    i, fr = take()
                    m = mm(bank[i][:], wpl[:, 128 * s_:128 * s_ + 128], up[:, 16:16 + T], True, True, fr, tp, t_wp,
                           mark=True)
                    bfree[i] = t_pool = act(mx[:, 4 + s_, :], bank[i][:], ACT.Copy, m,
                                            scale=W["pscale"][:, s_:s_ + 1])
                wfree[wi] = P.last()
            wi, w, tw = weights(A["wv2"], 4096)
            for t in range(NT):
                i, fr = take()
                for k in range(8):
                    m = mm(bank[i][:], hT[:, k, 128 * t:128 * t + 128], w[:, 512 * k:512 * k + 512], k == 0, k == 7,
                           fr, tw, tu, mark=(k == 7))
                bfree[i] = t_v = act(vt[:, t, :], bank[i][:], ACT.Copy, m)
            wfree[wi] = P.last()
            i, fr = take()
            for t in range(NT):
                for k in range(8):
                    m = mm(bank[i][:, 8 * t:8 * t + 8], hT[:, k, 128 * t:128 * t + 128], wsm[:, 8 * k:8 * k + 8],
                           k == 0, k == 7, fr, t_ws, tu, mark=(k == 7))
            x3 = xx[:].rearrange("p (t h) -> p t h", t=4)
            vtt(x3, bank[i][:, 0:32].rearrange("p (t h) -> p t h", t=4), bmid(W["bf"], 4), ADD, m)
            bfree[i] = vts(xx[:], xx[:], -1.0, None, MUL)
            lff = lf[:].rearrange("p t h -> p (t h)")
            softplus(lff, xx[:], [q_[:] for q_ in sp])
            t_lf = V.last()
            i, fr = take()
            for t in range(NT):
                for jt in range(t + 1):
                    m = mm(bank[i][:, 8 * t:8 * t + 8], ut if jt == t else ones, lf[:, jt, :], jt == 0, jt == t,
                           fr, t_lf, mark=(jt == t))
            bfree[i] = vts(cq[:].rearrange("p t h -> p (t h)"), bank[i][:, 0:32], -1.0, None, MUL, None, m)
            for h in range(8):
                i, fr = take()
                for kt in range(NT):
                    for jt in range(kt + 1):
                        m = mm(bank[i][:, 128 * kt:128 * kt + 128],
                               lf[:, jt, h:h + 1].to_broadcast([128, 128]), ut if jt == kt else ones,
                               jt == 0, jt == kt, fr, mark=(jt == kt))
                bfree[i] = t_cb = act(cb[h][:], bank[i][:], ACT.Copy, m, V.last())
            u_ = 0
            for t in range(NT):
                kn = 128 * (t + 1)
                t_ao = P.last()
                io, fro = take()
                for h in range(8):
                    b = u_ % 2
                    u_ += 1
                    i, fr = take()
                    if i == io:
                        i, fr = take()
                    hp = 64 * (h % 2)
                    ps = bank[i]
                    mm(ps[:, 0:kn], qk[hp:hp + 64, h // 2, 128 * t:128 * t + 128], qk[hp:hp + 64, 4 + h // 2, 0:kn],
                       True, False, fr, t_qk)
                    m = mm(ps[:, kn - 128:kn], ident, neg, False, True, mark=True)
                    lgb = lg[b]
                    vtt(lgb[:, 0:kn], ps[:, 0:kn], cb[h][:, 0:kn], ADD, m, t_cb, P.last())
                    bfree[i] = V.last()
                    red(mxx[:, b:b + 1], lgb[:, 0:kn], ALU.max)
                    vtt(mxx[:, 2 + b:3 + b], mxx[:, b:b + 1], cq[:, t, h:h + 1], ADD)
                    tb = vtt(mxx[:, 4 + b:5 + b], cq[:, t, h:h + 1], mxx[:, 2 + b:3 + b], SUB)
                    te_ = act(lgb[:, 0:kn], lgb[:, 0:kn], ACT.Exp, tb, bias=mxx[:, 4 + b:5 + b],
                              accum_out=den[:, h:h + 1])
                    i, fr = take()
                    if i == io:
                        i, fr = take()
                    for kt in range(t + 1):
                        m = tr(bank[i][:, 128 * kt:128 * kt + 128], lgb[:, 128 * kt:128 * kt + 128], ident, fr, te_,
                               mark=(kt == t))
                    bfree[i] = tp = copy(pT[b][:, 0:kn], bank[i][:, 0:kn], m, P.last())
                    for kt in range(t + 1):
                        m = mm(bank[io][:, 64 * h:64 * h + 64], pT[b][:, 128 * kt:128 * kt + 128],
                               vt[:, kt, 64 * h:64 * h + 64], kt == 0, kt == t, tp, t_v, fro, mark=(kt == t))
                recip(den[:], den[:], te_)
                ta = vtt(ao[:].rearrange("p (h e) -> p h e", h=8), bank[io][:].rearrange("p (h e) -> p h e", h=8),
                         b3(den[:], 64), MUL, m, t_ao)
                bfree[io] = ta
                i, fr = take()
                for k in range(4):
                    m = tr(bank[i][:, 128 * k:128 * k + 128], ao[:, 128 * k:128 * k + 128], ident, fr, ta,
                           mark=(k == 3))
                bfree[i] = t_at = act(mx[:, 0:4, 128 * t:128 * t + 128],
                                      bank[i][:].rearrange("p (k e) -> p k e", k=4), ACT.Copy, m, V.last())
            for hf in range(2):
                wi, w, tw = weights(A["wout2"][hf], 4096)
                for t in range(NT):
                    i, fr = take()
                    for k in range(8):
                        m = mm(bank[i][:], mx[:, k, 128 * t:128 * t + 128], w[:, 512 * k:512 * k + 512],
                               k == 0, k == 7, fr, tw, t_at, t_pool, mark=(k == 7))
                    hs = h2[:, t, 512 * hf:512 * hf + 512]
                    bfree[i] = vtt(hs, hs, bank[i][:], ADD, m)
                wfree[wi] = P.last()
            f = fence()

        with ExitStack() as pa:
            ab = lambda n, s, d=F32: sbx(pa, n, s, d)
            hT = ab("hT2", [128, 8, T])
            fT = ab("fT", [128, 22, T])
            row = ab("rowf", [128, 1024])
            ob = [ab(f"ob{i}", [128, 1024]) for i in range(2)]
            gs = [ab(f"gs{i}", [128, T]) for i in range(2)]
            t_row = load("l_row3", row[:], A["fing"], f)
            tu = turned(hT, W["n2"], f)
            for j in range(22):
                if j % 2 == 0:
                    wi, w, tw = weights(A["wgu"][j // 2], 4096)
                o = 2048 * (j % 2)
                ps = []
                for q_ in range(2):
                    i, fr = take()
                    for k in range(8):
                        m = mm(bank[i][:], w[:, o + q_ * 1024 + k * 128:o + q_ * 1024 + k * 128 + 128], hT[:, k, :],
                               k == 0, k == 7, fr, tw, tu, mark=(k == 7))
                    ps.append((i, m))
                if j % 2 == 1:
                    wfree[wi] = P.last()
                i, m = ps[0]
                bfree[i] = ta = act(gs[j % 2][:], bank[i][:], ACT.Silu, m, V.last())
                i, m = ps[1]
                bfree[i] = t_f = vtt(fT[:, j, :], gs[j % 2][:], bank[i][:], MUL, m, ta)
            for hf in range(2):
                if bn[0] % 8 not in (0, 4):
                    bn[0] += 4 - bn[0] % 4
                i, fr = take(4)
                for cidx, (k0, kn) in enumerate(((0, 11), (11, 11))):
                    wi, w, tw = weights(A["wdn"][hf, :, 512 * k0:512 * (k0 + kn)], 512 * kn)
                    for k in range(k0, k0 + kn):
                        for t in range(NT):
                            m = mm(bank[i + t][:], fT[:, k, 128 * t:128 * t + 128],
                                   w[:, 512 * (k - k0):512 * (k - k0) + 512], k == 0, k == 21, fr, tw, t_f,
                                   mark=(t == 3 and k == k0 + kn - 1) or k == 21)
                    wfree[wi] = P.last()
                for t in range(NT):
                    hs = h2[:, t, 512 * hf:512 * hf + 512]
                    bfree[i + t] = th = vtt(hs, hs, bank[i + t][:], ADD, m)
            for t in range(NT):
                tt = act(junk[:], h2[:, t, :], ACT.Square, th, accum_out=sm[:, t:t + 1])
            rsqrt(sm[:, 8:12], sm[:, 0:4], (sm[:, 16:20], sm[:, 24:28]), 1.0 / 1024, tt)
            ol = [lane(f"ol{i}") for i in range(2)]
            od = [None, None]
            o_dst = out.rearrange("(t p) d -> t p d", p=128)
            for t in range(NT):
                tk = stt(ob[t % 2][:], h2[:, t, :], sm[:, 8 + t:9 + t], row[:], MUL, MUL, t_row, od[t % 2])
                od[t % 2] = store(ol[t % 2], o_dst[t], ob[t % 2][:], tk)
            D.waits(od)

        block = ctx.enter_context(nc.Block())
        block.sync(lambda e: D.emit(e))
        block.gpsimd(lambda e: Gp.emit(e))
        block.vector(lambda e: V.emit(e))
        block.scalar(lambda e: S.emit(e))
        block.tensor(lambda e: P.emit(e))


def laid_out(i):
    c = np.ascontiguousarray
    f = {k: np.asarray(v) for k, v in i.items()}
    w = f["w_in"][0].reshape(8, 128, 11296)

    def tiles(m, cols, kt):
        return m[:, :, cols].transpose(1, 0, 2).reshape(128, -1)

    def rows(v):
        return np.broadcast_to(v.reshape(1, -1), (128, v.size))

    def fm(v, n):
        return v.reshape(n, 128).T

    r = np.arange
    o = {}
    o["x"] = c(f["x"][0])
    o["meta"] = c(f["meta_tokens"])
    o["wdt"] = c(tiles(w, r(6144, 6176), 8))
    o["wg"] = c(np.stack([tiles(w, np.concatenate([2048 + 256 * g + r(256), 4096 + 128 * g + r(128),
                                                   5120 + 128 * g + r(128), 256 * g + r(256)]), 8) for g in range(8)]))
    o["wsc"] = c(np.stack([tiles(w, np.concatenate([6176 + 128 * j + r(128), 7200 + 128 * j + r(128),
                                                    8224 + 128 * j + r(128)]), 8) for j in range(8)]))
    wo_ = f["ssd_w_out"][0].reshape(16, 128, 1024)
    so_ = f["sc_w_out"][0].reshape(8, 128, 1024)
    o["wgo"] = c(np.stack([np.concatenate([
        tiles(w, 9248 + 128 * j + r(128), 8), tiles(w, 10272 + 128 * j + r(128), 8),
        tiles(wo_, 128 * j + r(128), 16), tiles(so_, 128 * j + r(128), 8)], 1) for j in range(8)]))
    w2 = f["w_o"][0].reshape(8, 128, 1024)
    o["wo"] = c(np.stack([tiles(w2, 512 * j + r(512), 8) for j in range(2)]))
    wq = f["peer_w_q"][0].reshape(8, 128, 2048)
    one = lambda m, n, k=1: np.stack([np.concatenate([tiles(m, 128 * (k * a + b) + r(128), 8) for b in range(k)], 1)
                                      for a in range(n)])
    o["wq"] = c(one(wq, 4, 4))
    o["keys"] = c(f["peer_sub_keys"][0].reshape(16, 128, 128).transpose(2, 0, 1).reshape(128, 2048))
    o["pu"] = c(f["peer_u"][0])
    o["pv"] = c(f["peer_v"][0])
    o["lnffn"] = c(rows(f["ln_ffn"][0]))
    o["lnfin"] = c(rows(f["ln_final"]))
    o["fing"] = c(rows(f["final_g_2"]))
    wi2 = f["w_in_2"][0]
    wi2 = wi2.reshape(8, 128, 2056)
    o["wqku"] = c(np.stack([np.concatenate([tiles(wi2, b + 128 * q + r(128), 8) for q in range(4)], 1)
                            for b in (0, 512, 1544)]))
    o["wv2"] = c(tiles(wi2, 1024 + r(512), 8))
    o["wf2"] = c(tiles(wi2, 1536 + r(8), 8))
    o["wpool"] = c(f["w_pool_2"][0].transpose(1, 0, 2).reshape(128, 512))
    wo2 = f["w_out_2"][0].reshape(8, 128, 1024)
    o["wout2"] = c(np.stack([tiles(wo2, 512 * j + r(512), 8) for j in range(2)]))
    wg, wu = f["w_gate_2"][0].reshape(8, 128, 2816), f["w_up_2"][0].reshape(8, 128, 2816)
    o["wgu"] = c(np.stack([np.concatenate([tiles(m, 128 * j + r(128), 8) for j in (2 * a, 2 * a + 1)
                                           for m in (wg, wu)], 1) for a in range(11)]))
    wd = f["w_down_2"][0].reshape(22, 128, 1024)
    o["wdn"] = c(np.stack([tiles(wd, 512 * j + r(512), 22) for j in range(2)]))
    cw, cb = f["ssd_conv_w"][0], f["ssd_conv_b"][0]
    idx = [a + r(128) for g in range(8) for a in (256 * g, 256 * g + 128, 2048 + 128 * g, 3072 + 128 * g)]
    v = {"lnmix": fm(f["ln_mix"][0], 8), "convw": np.concatenate([cw[q] for q in idx], 1),
         "convb": np.stack([cb[q] for q in idx], 1), "dskip": fm(np.repeat(f["ssd_d"][0], 64), 16),
         "normg": fm(f["ssd_norm"][0], 16),
         "scw": f["sc_conv_w"][0].reshape(8, 128, 3).transpose(1, 0, 2).reshape(128, 24),
         "dtb": rows(f["ssd_dt_bias"][0]), "alog": rows(f["ssd_a_log"][0]), "n1": fm(f["norm1_g_2"][0], 8),
         "n2": fm(f["norm2_g_2"][0], 8), "bf": rows(f["b_forget_2"][0]), "pscale": fm(f["pool_scale_2"][0], 4)}
    o["vec"] = c(np.concatenate([v[k] for k in VEC], 1))
    p, q = np.meshgrid(r(128), r(128), indexing="ij")
    one_ = np.float32(1)
    rc = np.concatenate([1.0 / np.minimum(r(16) + 1, 2 << s) for s in range(4)])
    o["con"] = c(np.concatenate([(p == q) * one_, (p <= q) * one_, (p > q) * one_, (p < q) * np.float32(-1e30),
                                 np.ones((128, 128)), np.broadcast_to(r(16)[None], (128, 16)),
                                 np.broadcast_to(rc[None], (128, 64))], 1).astype(np.float32))
    return o


def kernel(**inputs):
    import concourse.bacc as bacc
    from concourse.bass_utils import run_bass_kernel_spmd

    nc = bacc.Bacc("TRN2", target_bir_lowering=False, num_devices=1)
    arrays = laid_out(inputs)
    A = {k: nc.dram_tensor("in_" + k, a.shape, F32, kind="ExternalInput").ap() for k, a in arrays.items()}
    out = nc.dram_tensor("out_0", (T, 1024), F32, kind="ExternalOutput").ap()
    build(nc, A, out)
    r = run_bass_kernel_spmd(nc, [{"in_" + k: a for k, a in arrays.items()}], core_ids=[0])
    return r.results[0]["out_0"].reshape(1, T, 1024)
```

```python
from contextlib import ExitStack

import numpy as np
import concourse.bass as bass
from concourse import mybir

F32 = mybir.dt.float32
U32 = mybir.dt.uint32
ALU = mybir.AluOpType
ACT = mybir.ActivationFunctionType
AX = mybir.AxisListType
MUL, ADD, SUB = ALU.mult, ALU.add, ALU.subtract

T = 512
NT = 4
META = 16
L = META + T
WSLOT = 3072
G = 8
NEG = -3.0e38


class Queue:

    def __init__(self, sem, chain):
        self.sem, self.chain, self.n, self.items, self.seen = sem, chain, 0, [], {}
        self.cost = 0.0
        self.stream, self.tail, self.base = "main", {}, None

    def waits(self, after):
        need = {}

        def walk(x):
            if x is None:
                return
            if isinstance(x, tuple) and len(x) == 2 and isinstance(x[1], int):
                s, v = x
                if need.get(id(s), (s, 0))[1] < v:
                    need[id(s)] = (s, v)
            else:
                for y in x:
                    walk(y)

        walk(after)
        for k, (s, v) in need.items():
            if self.seen.get(k, 0) < v:
                self.seen[k] = v
                self.items.append(("wait", s, v))

    def __call__(self, fn, *after, mark=True):
        if self.chain:
            back = self.tail.get(self.stream, 0) if self.base is None else self.base
            if back:
                after = after + ((self.sem, back),)
        self.waits(after)
        if mark:
            self.n += 1
            self.tail[self.stream] = self.n
            self.items.append(("op", fn, self.sem, 1))
            return (self.sem, self.n)
        self.items.append(("op", fn, None, 0))
        return None

    def last(self):
        return (self.sem, self.tail.get(self.stream, 0) if self.chain else self.n)

    def apart(self, to=None):
        self.base = self.tail.get(self.stream, 0) if to is None else to

    def together(self):
        self.base = None

    def emit(self, eng):
        for it in self.items:
            if it[0] == "wait":
                eng.wait_ge(it[1], it[2])
            else:
                ins = it[1](eng)
                if it[2] is not None:
                    ins.then_inc(it[2], it[3])


class Lane:

    def __init__(self, sem):
        self.sem, self.n = sem, 0

    def start(self, queue, fn, *after):
        queue.waits((after, (self.sem, self.n) if self.n else None))
        self.n += 16
        queue.items.append(("op", fn, self.sem, 16))
        return (self.sem, self.n)


def b3(ap, n):
    return ap.unsqueeze(2).to_broadcast([ap.shape[0], ap.shape[1], n])


def bmid(ap, n):
    return ap.unsqueeze(1).to_broadcast([ap.shape[0], n, ap.shape[1]])


VEC = {}
_o = 0
for _k, _w in (("lnmix", 8), ("convw", 128), ("convb", 32), ("dskip", 16), ("normg", 16), ("scw", 24),
               ("dtb", 32), ("alog", 32), ("n1", 8), ("n2", 8), ("bf", 8), ("pscale", 4), ("lnffn", 8)):
    VEC[_k] = (_o, _o + _w)
    _o += _w
NVEC = _o
CON = {"ident": (0, 128), "ut": (128, 256), "sl": (256, 384), "neg": (384, 512), "ones": (512, 640),
       "iota": (640, 656), "rc": (656, 720)}
NCON = 720
NW = 3
NR = 8
ASPLIT = ((0, 2), (2, 4))
BSPLIT = (("attend", 0, 2), ("attend", 2, 3), ("feed", 0, 3), ("attend", 3, 4), ("feed", 3, 4))
EW = (1.5, 1.6, 1.3, 2.0)
VW = 1.5
SX = 1.6
AW = 1.6
AW0 = 2.8
CW = (1.0, 1.0)


def build(nc, A, out):
    ctx = ExitStack()
    with ctx:
        sem = lambda n: ctx.enter_context(nc.semaphore(n))
        sbx = lambda cx, n, s, d=F32: cx.enter_context(nc.sbuf_tensor(n, s, d))
        sb = lambda n, s, d=F32: sbx(ctx, n, s, d)
        V, S, P, Gp, D = (Queue(sem("s_dve"), True), Queue(sem("s_act"), True), Queue(sem("s_pe"), False),
                          Queue(sem("s_pool"), True), Queue(sem("s_sp"), False))
        lane = lambda n: Lane(sem(n))

        con = sb("con", [128, NCON])
        vec = sb("vec", [128, NVEC])
        C = {k: con[:, a:b] for k, (a, b) in CON.items()}
        W = {k: vec[:, a:b] for k, (a, b) in VEC.items()}
        ident, ut, sl, neg, ones = C["ident"], C["ut"], C["sl"], C["neg"], C["ones"]
        h2 = sb("h2", [128, NT, 1024])
        wdt = sb("wdt", [128, 256])
        wsm = sb("wsm", [128, 64])
        wpl = sb("wpl", [128, 512])
        rowa = sb("rowa", [128, 1024])
        rowb = sb("rowb", [128, 1024])
        wr = [sb(f"wr{i}", [128, WSLOT]) for i in range(NW)]
        sm = sb("sm", [128, 96])
        se = sb("se", [128, 16])
        rs2 = sb("rs2", [128, NT])
        junk = sb("junk", [128, 1024])
        eidx = sb("eidx", [128, NT, 128], U32)
        gate = sb("gate", [128, NT, 128])
        ring = [sb(f"ring{i}", [128, 1024]) for i in range(NR)]
        u2 = sb("u2", [128, 1024])
        junke = sb("junke", [128, 1024])
        acc = sb("acc", [128, 1024])
        dots = sb("dots", [128, 128])
        wgt = sb("wgt", [128, 128])
        st = sb("st", [128, G, 256])
        hist = sb("hist", [128, 32, 3])
        hsc = sb("hsc", [128, 8, 2])
        aneg = sb("aneg", [128, 32])
        bank = [ctx.enter_context(nc.psum_tensor(f"ps{i}", [128, 512], F32)) for i in range(8)]

        bfree = [None] * 8
        wlane, wfree, wn = [lane(f"wl{i}") for i in range(NW)], [None] * NW, [0]
        rl, rf = [lane(f"rl{i}") for i in range(NR)], [None] * NR
        turn = {"lo": 0, "hi": 0}

        def take(which="lo"):
            i = turn[which] % 4 + (4 if which == "hi" else 0)
            turn[which] += 1
            return i, bfree[i]

        def fence():
            return [q.last() for q in (V, S, P) if q.n]

        def weights(src, n, *after):
            i = wn[0] % NW
            wn[0] += 1
            tok = wlane[i].start(D, lambda e: e.dma_start(wr[i][:, 0:n], src), wfree[i], after)
            return i, wr[i], tok

        def size(ap):
            n = 1
            for x in ap.shape[1:]:
                n *= x
            return n

        def mm(o, l, r, start, stop, *after, mark=False):
            P.cost += max(64, size(r)) / 600.0
            return P(lambda e: e.matmul(o, l, r, start=start, stop=stop, skip_group_check=True), *after, mark=mark)

        def tr(o, i, idn, *after, mark=False):
            P.cost += 0.12
            return P(lambda e: e.transpose(o, i, idn), *after, mark=mark)

        def vts(o, i, a, b, o0, o1=None, *after):
            V.cost += 0.07 + size(i) / 1500.0
            return V(lambda e: e.tensor_scalar(o, i, a, b, o0, **({} if o1 is None else {"op1": o1})), *after)

        def vtt(o, a, b, op, *after):
            V.cost += 0.07 + size(a) / 960.0
            return V(lambda e: e.tensor_tensor(o, a, b, op), *after)

        def stt(o, a, s, b, op0, op1, *after):
            V.cost += 0.07 + size(a) / 960.0
            return V(lambda e: e.scalar_tensor_tensor(out=o, in0=a, scalar=s, in1=b, op0=op0, op1=op1), *after)

        def act(o, i, f, *after, **kw):
            return S(lambda e: e.activation(o, i, f, **kw), *after)

        def copy(o, i, *after):
            V.cost += 0.07 + size(i) / 960.0
            return V(lambda e: e.tensor_copy(o, i), *after)

        def mset(o, v, *after):
            return V(lambda e: e.memset(o, v), *after)

        def recip(o, i, *after):
            return V(lambda e: e.reciprocal(o, i), *after)

        def red(o, i, op, *after):
            V.cost += 0.07 + size(i) / 960.0
            return V(lambda e: e.tensor_reduce(o, i, AX.X, op), *after)

        def side_by_side(*parts):
            start = V.tail.get(V.stream, 0)
            home, live = V.stream, list(enumerate(parts))
            for q, _ in live:
                V.tail[q] = start
            while live:
                for q, p_ in list(live):
                    V.stream = q
                    if next(p_, None) is None:
                        live.remove((q, p_))
            V.stream = home
            V.tail[home] = max(V.tail[q] for q in range(len(parts)))

        def load(name, o, src, *after):
            return lane(name).start(D, lambda e: e.dma_start(o, src), *after)

        def store(ln, o, src, *after):
            return ln.start(S, lambda e: e.dma_start(o, src), *after)

        def rsqrt(o, ss, tmp, inv_n, *after):
            v, a = tmp
            t = vts(v, ss, inv_n, 1e-6, MUL, ADD, *after)
            t = act(a, v, ACT.Ln, t)
            t = act(a, a, ACT.Exp, scale=-0.5)
            vtt(o, a, a, MUL, t)
            vtt(o, o, v, MUL)
            vts(o, o, -0.5, 1.5, MUL, ADD)
            return vtt(o, o, a, MUL)

        def softplus(o, x, tmp, *after):
            e, w, l = tmp
            vts(l, x, -1.0, None, MUL, None, *after)
            t = vtt(l, l, x, ALU.min)
            t = act(e, l, ACT.Exp, t)
            t = vts(w, e, 1.0, None, ADD, None, t)
            t = act(l, w, ACT.Ln, t)
            vts(w, w, -1.0, None, ADD, None, t)
            vts(o, w, 0.0, None, ALU.is_equal)
            vtt(l, l, o, ADD)
            vtt(w, w, o, ADD)
            recip(w, w)
            vtt(l, l, w, MUL)
            vtt(l, l, e, MUL)
            vts(o, x, 0.0, None, ALU.max)
            return vtt(o, o, l, ADD)

        def merge(*streams):
            live = [[0.0, s, x] for s, x in streams if s is not None]
            while live:
                one = min(live, key=lambda x: x[0])
                p, v = P.cost, V.cost
                if next(one[1], None) is None:
                    live.remove(one)
                    continue
                one[0] += max(P.cost - p, V.cost - v) + one[2]
                yield True

        t_x = [load(f"l_x{t}", h2[:, t, :], A["x"][128 * t:128 * t + 128, :]) for t in range(2)]
        xm = ring[NR - 1][0:16, :]
        t_xm = load("l_xm", xm, A["meta"])
        t_con = load("l_con", con[:], A["con"])
        t_vec = load("l_vec", vec[:], A["vec"])
        t_wdt = load("l_wdt", wdt[:], A["wdt"])
        got = {}

        def mixer(t0, t1):
            nt = t1 - t0
            m0 = META if t0 == 0 else 0
            n = m0 + 128 * nt
            nr = 128 * nt
            chunks = ([(0, 16, None)] if m0 else []) + [(m0 + 128 * c, 128, c) for c in range(nt)]
            nc_ = len(chunks)
            f = fence()
            with ExitStack() as pa:
                ab = lambda nm, s, d=F32: sbx(pa, f"{nm}_{t0}", s, d)
                uT = ab("uT", [128, 8, n])
                scT = ab("scT", [128, 8, nr])
                yh = ab("yh", [128, nt, 2048])
                mg = yh[:].rearrange("p a b -> p (a b)")[:, 0:8 * nr].rearrange("p (k n) -> p k n", k=8)
                ss = ab("ss", [128, nt, 8])
                rs = [ab(f"rs{i}", [128, nt * 8]) for i in range(3)]
                pb = ExitStack()
                ab = lambda nm, s, d=F32: sbx(pb, f"{nm}_{t0}", s, d)
                xp = [ab(f"xp{i}", [128, 3 + n]) for i in range(3)]
                xs_ = ab("xs_", [128, n])
                xpf = [None] * 3
                xc = [ab(f"xc{i}", [128, 4, n]) for i in range(2)]
                zs = [ab(f"zs{i}", [128, nt, 256]) for i in range(2)]
                dD = [ab(f"dD{i}", [128, 2, 128]) for i in range(2)]
                dt, av, ac, ea, te, et = [ab(k, [128, nc_, 32]) for k in ("dt", "av", "ac", "ea", "te", "et")]
                sp = [ab(f"sp{i}", [128, 32 * nc_]) for i in range(3)]
                xdt = [ab(f"xdt{i}", [128, 256]) for i in range(nc_)]
                xw = [ab(f"xw{i}", [128, 256]) for i in range(nc_)]
                btm = [ab(f"btm{i}", [128, 128]) for i in range(nc_)]
                sla = [ab(f"sla{i}", [128, 4, 128]) for i in range(nt)]
                mt = ab("mt", [128, nt, 4, 128])
                cbm = [ab(f"cbm{i}", [128, 128]) for i in range(nt)]
                tmpx = [ab(f"tmpx{i}", [128, n]) for i in range(2)]
                tmpy = ab("tmpy", [128, nr])
                cnt = [0]
                srcs = [(h2[:, t0 + t, :], 128, m0 + 128 * t, t_x[t0 + t]) for t in range(nt)]
                if m0:
                    srcs.append((xm, 16, 0, t_xm))
                mset(sm[:], 1.0, f)
                for q, (src, w_, col, tk) in enumerate(srcs):
                    tt = act(junk[0:w_, :], src, ACT.Square, f, tk, V.last(), P.last() if P.n else None,
                             accum_out=sm[0:w_, q:q + 1])
                rsqrt(sm[:, 8:12], sm[:, 0:4], (sm[:, 16:20], sm[:, 24:28]), 1.0 / 1024, tt)
                V.apart()
                tk = [vts(junk[:, 128 * q:128 * q + 128], ident, sm[:, 8 + q:9 + q], None, MUL, None, t_con)
                      for q in range(len(srcs))]
                V.together()
                for q, (src, w_, col, _) in enumerate(srcs):
                    for kk in (0, 4):
                        i, fr = take()
                        for k in range(kk, kk + 4):
                            m = mm(bank[i][:, (k - kk) * 128:(k - kk) * 128 + w_], src[:, k * 128:(k + 1) * 128],
                                   junk[0:w_, 128 * q:128 * q + w_], True, True, fr, tk, mark=(k == kk + 3))
                        S.apart()
                        for k in range(kk, kk + 4):
                            tu = act(uT[:, k, col:col + w_], bank[i][:, (k - kk) * 128:(k - kk) * 128 + w_], ACT.Copy,
                                     m, t_vec, scale=W["lnmix"][:, k:k + 1])
                        S.together()
                        bfree[i] = tu
                    yield True
                if m0:
                    ta = act(aneg[:], W["alog"], ACT.Exp, t_vec)
                    vts(aneg[:], aneg[:], -1.0, None, MUL, None, ta)
                mset(dt[:], 0.0)
                i, fr = take()
                for c, (col, w_, _) in enumerate(chunks):
                    for k in range(8):
                        m = mm(bank[i][0:w_, 32 * c:32 * c + 32], uT[:, k, col:col + w_], wdt[:, 32 * k:32 * k + 32],
                               k == 0, k == 7, tu, fr, t_wdt, mark=(k == 7))
                for c, (col, w_, _) in enumerate(chunks):
                    td = vtt(dt[0:w_, c, :], bank[i][0:w_, 32 * c:32 * c + 32], W["dtb"][0:w_, :], ADD, m)
                bfree[i] = td
                dflat, aflat = dt[:].rearrange("p c h -> p (c h)"), av[:].rearrange("p c h -> p (c h)")
                softplus(aflat, dflat, [x[:] for x in sp])
                copy(dflat, aflat)
                ta = vtt(av[:], dt[:], bmid(aneg[:], nc_), MUL)
                i, fr = take()
                for c, (col, w_, _) in enumerate(chunks):
                    mm(bank[i][0:w_, 32 * c:32 * c + 32], ut[0:w_, 0:w_], av[0:w_, c, :], c == 0, True, ta, fr)
                for c, (col, w_, _) in enumerate(chunks):
                    m = mm(bank[i][:, 256 + 32 * c:288 + 32 * c], ones[0:w_, :], av[0:w_, c, :], False, True, mark=True)
                mset(te[:], 0.0)
                for c, (col, w_, _) in enumerate(chunks):
                    copy(ac[0:w_, c, :], bank[i][0:w_, 32 * c:32 * c + 32], m)
                    t1 = vtt(te[0:w_, c, :], bank[i][0:w_, 256 + 32 * c:288 + 32 * c], ac[0:w_, c, :], SUB)
                for c, (col, w_, _) in enumerate(chunks):
                    act(ea[0:w_, c, :], ac[0:w_, c, :], ACT.Exp, t1)
                    act(te[0:w_, c, :], te[0:w_, c, :], ACT.Exp)
                    t_dec = act(et[:, c, :], bank[i][:, 256 + 32 * c:288 + 32 * c], ACT.Exp)
                bfree[i] = t_dec
                yield True

                f_y = fence()

                def conv_in(hst, width):
                    b = cnt[0] % 3
                    cnt[0] += 1
                    if m0:
                        tk = mset(xp[b][:, 0:width], 0.0, xpf[b])
                    else:
                        tk = copy(xp[b][:, 0:width], hst, xpf[b])
                    return b, xp[b], tk

                def short_units(j):
                    k_ = {}

                    def product(s_):
                        if s_ == 2:
                            k_["w"] = weights(A["wsc"][j], 3072)
                        wi, w, tw = k_["w"]
                        off = m0 if s_ == 0 else 0
                        i, fr = take()
                        for k in range(8):
                            m = mm(bank[i][:, 0:n - off], w[:, k * 384 + s_ * 128:k * 384 + s_ * 128 + 128],
                                   uT[:, k, off:n], k == 0, k == 7, fr, tw, tu, mark=(k == 7))
                        if s_ == 0:
                            wfree[wi] = m
                        k_[s_] = (i, m)

                    def keep_x():
                        i, m = k_[2]
                        bfree[i] = k_["x"] = act(xs_[:], bank[i][:, 0:n], ACT.Copy, m, got.get("xs_"), f)

                    def times():
                        i, m = k_[1]
                        b, x, _ = conv_in(hsc[:, j, :], 2)
                        bfree[i] = got["xs_"] = vtt(x[:, 2:2 + n], bank[i][:, 0:n], xs_[:], MUL, k_["x"], m)
                        copy(hsc[:, j, :], x[:, n:n + 2])
                        sw, cv = W["scw"], tmpy[:, 0:nr]
                        vts(cv, x[:, m0:m0 + nr], sw[:, 3 * j:3 * j + 1], None, MUL)
                        for k in (1, 2):
                            xpf[b] = stt(cv, x[:, m0 + k:m0 + k + nr], sw[:, 3 * j + k:3 * j + k + 1], cv, MUL, ADD)

                    def finish():
                        i, m = k_[0]
                        bfree[i] = vtt(scT[:, j, :], bank[i][:, 0:nr], tmpy[:, 0:nr], MUL, m)

                    return [(lambda: product(2), keep_x, None), (lambda: product(1), times, None),
                            (lambda: product(0), finish, None)]

                pe_done, v_done, cur = [None, None], [None, None], {}

                def group_units(g):
                    k_ = {}
                    xg = xc[g % 2]
                    cw = W["convw"]

                    def product(s_):
                        if s_ in (0, 3):
                            k_["w"] = weights(A["wg"][g, s_ // 3], 3072)
                        wi, w, tw = k_["w"]
                        so = 128 * s_ if s_ < 3 else 0
                        i, fr = take()
                        for k in range(8):
                            m = mm(bank[i][:, 0:n], w[:, k * 384 + so:k * 384 + so + 128], uT[:, k, :], k == 0, k == 7,
                                   fr, tw, tu, mark=(k == 7))
                        if s_ == 2:
                            wfree[wi] = m
                        k_[s_] = (i, m)

                    def convolve(s_):
                        i, m = k_[s_]
                        b, x, t_in = conv_in(hist[:, 4 * g + s_, :], 3)
                        bfree[i] = act(x[:, 3:3 + n], bank[i][:, 0:n], ACT.Copy, m, t_in)
                        q4 = (4 * g + s_) * 4
                        S.apart()
                        act(hist[:, 4 * g + s_, :], x[:, n:n + 3], ACT.Copy)
                        tx = act(tmpx[s_ % 2][:], x[:, 0:n], ACT.Copy, got.get(("tmpx", s_ % 2)), f,
                                 scale=cw[:, q4:q4 + 1])
                        S.together()
                        for k in range(1, 4):
                            tv = got[("tmpx", s_ % 2)] = stt(
                                tmpx[s_ % 2][:] if k < 3 else xg[:, s_, :], x[:, k:k + n], cw[:, q4 + k:q4 + k + 1],
                                tmpx[s_ % 2][:], MUL, ADD, tx, pe_done[g % 2] if k == 3 else None)
                        xpf[b] = k_[("v", s_)] = tv

                    def smooth(s_):
                        k_["xc"] = act(xg[:, s_, :], xg[:, s_, :], ACT.Silu, k_[("v", s_)],
                                       bias=W["convb"][:, 4 * g + s_:4 * g + s_ + 1])

                    def z_product():
                        wi, w, tw = k_["w"]
                        i, fr = take()
                        for c in range(nt):
                            for k in range(8):
                                m = mm(bank[i][:, 256 * c:256 * c + 256], uT[:, k, m0 + 128 * c:m0 + 128 * c + 128],
                                       w[:, k * 384 + 128:k * 384 + 384], k == 0, k == 7, fr, tw, mark=(k == 7))
                        wfree[wi] = m
                        k_["z"] = (i, m)

                    def z_keep():
                        i, m = k_["z"]
                        bfree[i] = k_["tz"] = act(zs[g % 2][:].rearrange("p a b -> p (a b)"), bank[i][:, 0:256 * nt],
                                                  ACT.Silu, m, v_done[g % 2], f)
                        for j in range(2):
                            k_["td"] = act(dD[g % 2][:, j, :], ident, ACT.Copy, pe_done[g % 2], f,
                                           scale=W["dskip"][:, 2 * g + j:2 * g + j + 1])

                    def ready():
                        cur[g] = (k_["xc"], k_["tz"], k_["td"])

                    def unit(s_):
                        return (lambda: product(s_), lambda: convolve(s_), lambda: smooth(s_))

                    return [unit(s_) for s_ in range(4)] + [(z_product, z_keep, ready)]

                def pipeline(units):
                    for q in range(len(units) + 2):
                        for lag in range(3):
                            if 0 <= q - lag < len(units) and units[q - lag][lag] is not None:
                                units[q - lag][lag]()
                        yield True

                def scan(g):
                    xg, zg, dg = xc[g % 2], zs[g % 2], dD[g % 2]
                    t_xc, t_z, t_d = cur[g]
                    free = got.get("scan")
                    real = [(c, col, q) for c, (col, w_, q) in enumerate(chunks) if q is not None]
                    tms, ts_, tx, tb, txw = {}, {}, {}, {}, {}

                    def slopes(c, q):
                        S.apart()
                        for h in range(4):
                            ts_[q] = act(sla[q][:, h, :], sl, ACT.Copy, ta, free, f,
                                         scale=av[:, c, 4 * g + h:4 * g + h + 1])
                        S.together()

                    def turn_chunk(c, col, w_):
                        i, fr = take("hi")
                        for s_ in range(3):
                            m = tr(bank[i][0:w_, s_ * 128:s_ * 128 + 128], xg[:, s_, col:col + w_], ident, fr, t_xc,
                                   mark=(s_ == 2))
                        return i, m

                    def keep_chunk(c, w_, i, m):
                        S.apart()
                        tb[c] = act(btm[c][0:w_, :], bank[i][0:w_, 256:384], ACT.Copy, m, free, f)
                        for h in range(4):
                            bfree[i] = tx[c] = act(xdt[c][0:w_, 64 * h:64 * h + 64], bank[i][0:w_, 64 * h:64 * h + 64],
                                                   ACT.Copy, ta, scale=dt[0:w_, c, 4 * g + h:4 * g + h + 1])
                        S.together()
                        txw[c] = vtt(xw[c][0:w_, :].rearrange("p (h e) -> p h e", h=4),
                                     xdt[c][0:w_, :].rearrange("p (h e) -> p h e", h=4),
                                     b3(te[0:w_, c, 4 * g:4 * g + 4], 64), MUL, tx[c], t_dec)

                    for c, col, q in real:
                        slopes(c, q)
                    held = {}
                    for c, (col, w_, q) in enumerate(chunks):
                        held[c] = turn_chunk(c, col, w_)
                        yield True
                        if q is not None:
                            i, fr = take("hi")
                            for h in range(4):
                                m = mm(bank[i][:, 128 * h:128 * h + 128], sla[q][:, h, :], ut, h == 0, True, fr, ts_[q],
                                       mark=(h == 3))
                            held[("d", q)] = (i, m)
                        keep_chunk(c, w_, *held[c])
                        yield True
                        if q is not None:
                            i, m = held[("d", q)]
                            bfree[i] = tms[q] = act(mt[:, q].rearrange("p a b -> p (a b)"), bank[i][:], ACT.Exp, m,
                                                    free, f)
                    for c, col, q in real:
                        i, fr = take("hi")
                        m = mm(bank[i][:, 0:128], xg[:, 2, col:col + 128], xg[:, 3, col:col + 128], True, True, fr,
                               mark=True)
                        bfree[i] = vtt(cbm[q][:], bank[i][:, 0:128], ut, MUL, m)
                        tms[q] = vtt(mt[:, q], mt[:, q], bmid(cbm[q][:], 4), MUL, tms[q])
                        if q == 0:
                            yield True
                    for c, (col, w_, q) in enumerate(chunks):
                        i2, fr = take("hi")
                        m2 = mm(bank[i2][:, 0:256], btm[c][0:w_, :], xw[c][0:w_, :], True, True, fr, txw[c], tb[c],
                                mark=True)
                        if q is not None:
                            yield True
                            i, fr = take("hi")
                            for j in range(2):
                                mm(bank[i][:, 128 * j:128 * j + 128], xg[:, j, col:col + w_], dg[:, j, :], j == 0,
                                   False, fr, t_d)
                            for h in range(4):
                                mm(bank[i][:, 64 * h:64 * h + 64], mt[:, q, h, :], xdt[c][:, 64 * h:64 * h + 64],
                                   False, False, tms[q], tx[c])
                            m = mm(bank[i][:, 256:512], xg[:, 3, col:col + w_], st[:, g, :], False, True,
                                   got[("st", g)], mark=True)
                            yield True
                            S.apart()
                            for h in range(4):
                                tst = act(st[:, g, 64 * h:64 * h + 64], st[:, g, 64 * h:64 * h + 64], ACT.Copy, m,
                                          got[("st", g)], scale=et[:, c, 4 * g + h:4 * g + h + 1])
                            yc = yh[:, q, 256 * g:256 * g + 256]
                            for h in range(4):
                                tyo = act(yc[:, 64 * h:64 * h + 64], bank[i][:, 256 + 64 * h:320 + 64 * h], ACT.Copy,
                                          m, f_y, scale=ea[:, c, 4 * g + h:4 * g + h + 1])
                            S.together()
                            bfree[i2] = got[("st", g)] = vtt(st[:, g, :], st[:, g, :], bank[i2][:, 0:256], ADD, tst, m2)
                            bfree[i] = vtt(yc, yc, bank[i][:, 0:256], ADD, tyo)
                            ty = v_done[g % 2] = vtt(yc, yc, zg[:, q, :], MUL, t_z)
                            yield True
                            got["ss"] = act(junk[:, 0:256], yc, ACT.Square, ty, accum_out=ss[:, q, g:g + 1])
                        else:
                            bfree[i2] = got[("st", g)] = copy(st[:, g, :], bank[i2][:, 0:256], m2)
                    pe_done[g % 2] = m
                    got["scan"] = [m, got[("st", g)]]

                for step in range(G + 1):
                    lead = (group_units(step) if step < G else []) + (short_units(step - 1) if step else [])
                    yield from merge((pipeline(lead), 0.001), (scan(step - 1) if step else None, SX))
                pb.close()
                f2 = fence()
                ynT = sbx(pa, f"ynT_{t0}", [128, 16, nr])
                g1 = sbx(pa, f"g1_{t0}", [128, 2, nr])
                t_sc = V.last()
                rsqrt(rs[0][:], ss[:].rearrange("p c g -> p (c g)"), (rs[1][:], rs[2][:]), 1.0 / 256, got["ss"])
                for c in range(nt):
                    yv = yh[:, c, :].rearrange("p (g e) -> p g e", g=8)
                    t_y = vtt(yv, yv, b3(rs[0][:, 8 * c:8 * c + 8], 256), MUL)
                for j in range(16):
                    i, fr = take(("lo", "hi")[j % 2])
                    for c in range(nt):
                        m = tr(bank[i][:, 128 * c:128 * c + 128], yh[:, c, 128 * j:128 * j + 128], ident, fr, t_y,
                               mark=(c == nt - 1))
                    bfree[i] = t_yn = act(ynT[:, j, :], bank[i][:, 0:nr], ACT.Copy, m, f2,
                                          scale=W["normg"][:, j:j + 1])
                    yield True
                t_free = P.last()
                for j in range(8):
                    wi, w, tw = weights(A["wgate"][j], 2048)
                    wi2, w2, tw2 = weights(A["wso"][j], 3072)
                    ps = []
                    for q_, (kn, rhs, wv, tv, base) in enumerate((
                            (8, uT, w, tw, 0), (8, uT, w, tw, 1024), (16, ynT, w2, tw2, 0), (8, scT, w2, tw2, 2048))):
                        i, fr = take(("lo", "hi")[j % 2])
                        off = m0 if q_ < 2 else 0
                        for k in range(kn):
                            m = mm(bank[i][:, 0:nr], wv[:, base + k * 128:base + k * 128 + 128],
                                   rhs[:, k, off:off + nr], k == 0, k == kn - 1, fr, tv, t_yn, t_sc,
                                   mark=(k == kn - 1))
                        if q_ == 1:
                            wfree[wi] = P.last()
                        ps.append((i, m))
                        yield True
                    wfree[wi2] = P.last()
                    for q_ in range(2):
                        i, m = ps[q_]
                        bfree[i] = tg = act(g1[:, q_, :], bank[i][:, 0:nr], ACT.Sigmoid, m, got.get("g1"), f2)
                    i, m = ps[2]
                    bfree[i] = vtt(g1[:, 0, :], g1[:, 0, :], bank[i][:, 0:nr], MUL, m, tg)
                    i, m = ps[3]
                    bfree[i] = vtt(g1[:, 1, :], g1[:, 1, :], bank[i][:, 0:nr], MUL, m)
                    got["g1"] = t_mg = vtt(mg[:, j, :], g1[:, 0, :], g1[:, 1, :], ADD, t_free)
                    yield True
                for hf in range(4):
                    wi, w, tw = weights(A["wo"][hf], 2048)
                    for t in range(nt):
                        i, fr = take()
                        for k in range(8):
                            m = mm(bank[i][:, 0:256], mg[:, k, 128 * t:128 * t + 128], w[:, 256 * k:256 * k + 256],
                                   k == 0, k == 7, fr, tw, t_mg, mark=(k == 7))
                        hv = h2[:, t0 + t, 256 * hf:256 * hf + 256]
                        bfree[i] = got["h2"] = vtt(hv, hv, bank[i][:, 0:256], ADD, m)
                        yield True
                    wfree[wi] = P.last()

        def turned(dst, gvec, t0, t1, rs_out, *after):
            for t in range(t0, t1):
                tt = act(junk[:], h2[:, t, :], ACT.Square, after, P.last(), V.last(), accum_out=sm[:, t:t + 1])
            nt = t1 - t0
            rsqrt(rs_out, sm[:, t0:t1], (sm[:, 16:16 + nt], sm[:, 24:24 + nt]), 1.0 / 1024, tt)
            V.apart()
            tk = [vts(junk[:, 128 * q:128 * q + 128], ident, rs_out[:, q:q + 1], None, MUL, None) for q in range(nt)]
            V.together()
            for t in range(t0, t1):
                for kk in (0, 4):
                    i, fr = take()
                    for k in range(kk, kk + 4):
                        m = mm(bank[i][:, (k - kk) * 128:(k - kk) * 128 + 128], h2[:, t, k * 128:(k + 1) * 128],
                               junk[:, 128 * (t - t0):128 * (t - t0) + 128], True, True, fr, tk, mark=(k == kk + 3))
                    S.apart()
                    for k in range(kk, kk + 4):
                        tu = act(dst[:, k, 128 * (t - t0):128 * (t - t0) + 128],
                                 bank[i][:, (k - kk) * 128:(k - kk) * 128 + 128], ACT.Copy, m, scale=gvec[:, k:k + 1])
                    S.together()
                    bfree[i] = got["turned"] = tu
                yield True

        def choose(t0, t1):
            nt = t1 - t0
            nr = 128 * nt
            f = fence()
            with ExitStack() as pa:
                bb = lambda nm, s, d=F32: sbx(pa, f"{nm}_{t0}", s, d)
                u2T = bb("u2T", [128, 8, nr])
                q_sb = [bb(f"q_sb{i}", [128, nr]) for i in range(2)]
                s_sb = bb("s_sb", [128, 16, nr])
                sv = bb("sv", [128, nt, 16, 16])
                si = bb("si", [128, nt, 16, 16], U32)
                sif = bb("sif", [128, nt, 16, 16])
                cand = bb("cand", [128, nt, 256])
                cv = bb("cv", [128, nt, 8, 16])
                ci = bb("ci", [128, nt, 8, 16], U32)
                cu = [bb(f"cu{i}", [128, 8, 16], U32) for i in range(2)]
                cx = [bb(f"cx{i}", [128, 8, 16]) for i in range(3)]
                oh = [bb(f"oh{i}", [128, 8, 256]) for i in range(2)]
                rd = bb("rd", [128, 8])
                t_s = [None] * 16

                def top16(v16, i16, x, tk):
                    for r_ in range(2):
                        v8, i8 = v16[:, 8 * r_:8 * r_ + 8], i16[:, 8 * r_:8 * r_ + 8]
                        V.cost += 0.1 + size(x) / 960.0
                        V(lambda e, v8=v8: e.max(v8, x), tk)
                        yield True
                        V.cost += 0.1 + size(x) / 960.0
                        V(lambda e, v8=v8, i8=i8: e.max_index(i8, v8, x))
                        yield True
                        if r_ == 0:
                            V.cost += 0.1 + size(x) / 960.0
                            V(lambda e, v8=v8: e.match_replace(out=x, in_to_replace=v8, in_values=x, imm_value=NEG))
                            yield True

                def pairs(t, h):
                    copy(sif[:, t, 2 * h:2 * h + 2, :], si[:, t, 2 * h:2 * h + 2, :])
                    yield True
                    vtt(cand[:, t, :].rearrange("p (a b) -> p a b", a=16), b3(sv[:, t, 2 * h, :], 16),
                        bmid(sv[:, t, 2 * h + 1, :], 16), ADD)
                    yield True
                    yield from top16(cv[:, t, h, :], ci[:, t, h, :], cand[:, t, :], None)

                yield from turned(u2T, W["lnffn"], t0, t1, rs2[:, t0:t1], f)
                tu = got["turned"]
                ws, qs = {}, {}

                def query(hj):
                    if hj % 2 == 0:
                        ws[hj // 2] = weights(A["wq"][hj // 2], 2304)
                    wi, w, tw = ws[hj // 2]
                    i, fr = take()
                    for k in range(8):
                        c0 = (hj % 2) * 1024 + k * 128
                        m = mm(bank[i][:, 0:nr], w[:, c0:c0 + 128], u2T[:, k, :], k == 0, k == 7, fr, tw, tu,
                               mark=(k == 7))
                    bfree[i] = qs[hj] = act(q_sb[hj % 2][:], bank[i][:, 0:nr], ACT.Copy, m, got.get(("qq", hj % 2)), f)

                def scores(hj):
                    wi, w, tw = ws[hj // 2]
                    i, fr = take("hi")
                    for t in range(nt):
                        m = mm(bank[i][:, 128 * t:128 * t + 128], q_sb[hj % 2][:, 128 * t:128 * t + 128],
                               w[:, 2048 + 128 * (hj % 2):2176 + 128 * (hj % 2)], t == 0, True, fr, qs[hj],
                               mark=(t == nt - 1))
                    got[("qq", hj % 2)] = m
                    if hj % 2 == 1:
                        wfree[wi] = P.last()
                    bfree[i] = t_s[hj] = act(s_sb[:, hj, :], bank[i][:, 0:nr], ACT.Copy, m, f)

                query(0)
                for hj in range(16):
                    if hj < 15:
                        query(hj + 1)
                        yield True
                    scores(hj)
                    yield True
                    if hj % 2:
                        h = hj // 2
                        side_by_side(*[top16(sv[:, t, hj - 1 + j, :], si[:, t, hj - 1 + j, :],
                                             s_sb[:, hj - 1 + j, 128 * t:128 * t + 128], t_s[hj - 1 + j])
                                       for t in range(nt) for j in range(2)])
                        yield True
                        side_by_side(*[pairs(t, h) for t in range(nt)])
                        yield True
                for t in range(nt):
                    i4 = sif[:, t].rearrange("p (h j) k -> p h j k", j=2)

                    def soft():
                        gt = gate[:, t0 + t, :].rearrange("p (h k) -> p h k", h=8)
                        red(rd[:], cv[:, t], ALU.max)
                        yield True
                        tg = vtt(gt, cv[:, t], b3(rd[:], 16), SUB)
                        tg = act(gate[:, t0 + t, :], gate[:, t0 + t, :], ACT.Exp, tg)
                        yield True
                        for _ in range(4):
                            yield True
                        red(rd[:], gt, ADD, tg)
                        yield True
                        recip(rd[:], rd[:])
                        yield True
                        vtt(gt, gt, b3(rd[:], 16), MUL)

                    def first_index():
                        vts(cu[0][:], ci[:, t], 4, None, ALU.logical_shift_right)
                        yield True
                        copy(cx[0][:], cu[0][:])
                        yield True
                        for hh in (0, 4):
                            o4 = oh[0][:, hh:hh + 4, :].rearrange("p h (a b) -> p (h a) b", b=16)
                            vtt(o4, b3(cx[0][:, hh:hh + 4, :].rearrange("p h k -> p (h k)"), 16),
                                bmid(C["iota"], 64), ALU.is_equal)
                            yield True
                            for h in range(hh, hh + 4):
                                q4 = oh[0][:, h, :].rearrange("p (a b) -> p a b", b=16)
                                vtt(q4, q4, bmid(i4[:, h, 0, :], 16), MUL)
                                yield True
                        red(cx[0][:].rearrange("p h k -> p (h k)"),
                            oh[0][:].rearrange("p h (a b) -> p (h a) b", b=16), ADD)

                    vts(cu[1][:], ci[:, t], 15, None, ALU.bitwise_and, None, got.get("pool_index"))
                    tk = copy(cx[1][:], cu[1][:])
                    for hh in (0, 4):
                        tk = vtt(oh[1][:, hh:hh + 4, :].rearrange("p h (a b) -> p (h a) b", b=16),
                                 b3(cx[1][:, hh:hh + 4, :].rearrange("p h k -> p (h k)"), 16),
                                 bmid(C["iota"], 64), ALU.is_equal)
                        for h in range(hh, hh + 4):
                            q4 = oh[1][:, h, :].rearrange("p (a b) -> p a b", b=16)
                            t_g = Gp(lambda e, q4=q4, s4=bmid(i4[:, h, 1, :], 16): e.tensor_tensor(q4, q4, s4, MUL), tk)
                    side_by_side(first_index(), soft())
                    yield True
                    got["pool_index"] = red(cx[1][:].rearrange("p h k -> p (h k)"),
                                            oh[1][:].rearrange("p h (a b) -> p (h a) b", b=16), ADD, t_g)
                    stt(cx[2][:], cx[0][:], 128.0, cx[1][:], MUL, ADD)
                    got[("e", t0 + t)] = copy(eidx[:, t0 + t, :], cx[2][:].rearrange("p h k -> p (h k)"))
                    done.add(("chosen", t0 + t))
                    yield True

        def gather(n, t, which, k):
            s_ = n % NR
            src = A[which]
            return rl[s_].start(Gp, lambda e: e.indirect_dma_start(
                ring[s_][:], None, src, bass.IndirectOffsetOnAxis(ap=eidx[:, t, k:k + 1], axis=0)),
                got[("e", t)], rf[s_])

        def dot(j_, a, b, o, *after):
            V.cost += 1.1
            return V(lambda e: e.tensor_tensor_reduce(j_, a, b, 1.0, 0.0, MUL, ADD, o), *after)

        def experts():
            jobs = [(t, w, k) for t in range(NT) for w in ("pu", "pv") for k in range(128)]
            toks = []

            def ahead(n):
                while len(toks) < min(n + NR, len(jobs)) and ("chosen", jobs[len(toks)][0]) in done:
                    toks.append(gather(len(toks), *jobs[len(toks)]))

            for n, (t, which, k) in enumerate(jobs):
                if which == "pu" and k == 0:
                    yield ("chosen", t)
                    if n == 0:
                        ahead(0)
                    tu = stt(u2[:], h2[:, t, :], rs2[:, t:t + 1], rowa[:], MUL, MUL, t_rowa, got[("e", t)])
                    past = [tu[1], tu[1]]
                if len(toks) <= n:
                    ahead(n)
                s_ = n % NR
                if which == "pu":
                    V.apart(past[-2])
                    rf[s_] = dot((junke, acc)[k % 2][:], ring[s_][:], u2[:], dots[:, k:k + 1], toks[n])
                    V.together()
                elif k == 0:
                    ta = act(wgt[:], dots[:], ACT.Gelu, V.last())
                    vtt(wgt[:], wgt[:], gate[:, t, :], MUL, ta)
                    rf[s_] = vts(acc[:], ring[s_][:], wgt[:, 0:1], None, MUL, None, toks[n])
                    past = [rf[s_][1] - 1] * 2
                else:
                    V.apart(past[-2])
                    if k == 1:
                        rf[s_] = vts(junke[:], ring[s_][:], wgt[:, 1:2], None, MUL, None, toks[n])
                    else:
                        a_ = (acc, junke)[k % 2]
                        rf[s_] = stt(a_[:], ring[s_][:], wgt[:, k:k + 1], a_[:], MUL, ADD, toks[n])
                    V.together()
                past.append(rf[s_][1])
                nx = len(toks)
                if nx < len(jobs) and nx == n + NR and ("chosen", jobs[nx][0]) in done:
                    toks.append(gather(nx, *jobs[nx]))
                if which == "pv" and k == 127:
                    vtt(acc[:], acc[:], junke[:], ADD)
                    th = vtt(h2[:, t, :], h2[:, t, :], acc[:], ADD)
                    tt = act(acc[:], h2[:, t, :], ACT.Square, th, accum_out=se[:, 0:1])
                    rsqrt(se[:, 1:2], se[:, 0:1], (se[:, 2:3], se[:, 3:4]), 1.0 / 1024, tt)
                    got[("h3", t)] = stt(h2[:, t, :], h2[:, t, :], se[:, 1:2], rowb[:], MUL, MUL, t_rowb)
                    done.add(("h3", t))
                yield EW[t]

        def attend(t0, t1, kv):
            pace[0] = AW if t0 else AW0
            kT, vt, cb, lf, uh = kv
            nt = t1 - t0
            nr = 128 * nt
            q0 = 128 * t0
            f = [fence(), got[("h3", t1 - 1)]]
            with ExitStack() as pa:
                ab = lambda nm, s, d=F32: sbx(pa, f"{nm}_{t0}", s, d)
                hT = ab("hT", [128, 8, nr])
                qT = ab("qT", [128, 4, nr])
                mx = ab("mx", [128, 8, nr])
                cq = ab("cq", [128, nt, 8])
                sp = [ab(f"sq{i}", [128, 8 * nt]) for i in range(3)]
                xx = ab("xx", [128, 8 * nt])
                lg = [ab(f"lg{i}", [128, T]) for i in range(2)]
                pT = [ab(f"pT{i}", [128, T]) for i in range(2)]
                up = ab("up", [128, 16 + nr])
                wb = [ab(f"wb{i}", [128, 16 + nr]) for i in range(2)]
                mxx = ab("mxx", [128, 16])
                den = ab("den", [128, 8])
                ao = ab("ao", [128, 512])
                yield from turned(hT, W["n1"], t0, t1, sm[:, 40:40 + nt], f)
                tu = got["turned"]
                for s3 in range(6):
                    wi, w, tw = weights(A["wqku"][s3], 2048)
                    for s_ in range(2):
                        i, fr = take()
                        for k in range(8):
                            m = mm(bank[i][:, 0:nr], w[:, s_ * 1024 + k * 128:s_ * 1024 + k * 128 + 128], hT[:, k, :],
                                   k == 0, k == 7, fr, tw, tu, mark=(k == 7))
                        j = 2 * (s3 % 2) + s_
                        yield True
                        if s3 < 2:
                            bfree[i] = act(qT[:, j, :], bank[i][:, 0:nr], ACT.Copy, m, f, scale=0.125)
                            continue
                        if s3 < 4:
                            bfree[i] = t_qk = act(kT[:, j, q0:q0 + nr], bank[i][:, 0:nr], ACT.Copy, m, f)
                            continue
                        if t0 == 0:
                            mset(up[:, 0:16], 0.0, P.last(), f)
                        else:
                            copy(up[:, 0:16], uh[:, j, :], P.last(), f)
                        bfree[i] = copy(up[:, 16:16 + nr], bank[i][:, 0:nr], m)
                        copy(uh[:, j, :], up[:, nr:nr + 16])
                        prev, d = up, 1
                        for lv in range(j + 1):
                            o = wb[lv % 2]
                            vtt(o[:, 2 * d - 1:16 + nr], prev[:, 2 * d - 1:16 + nr], prev[:, d - 1:16 + nr - d], ADD)
                            prev = o
                            d *= 2
                        pl = wb[(j + 1) % 2]
                        h_ = 0
                        if t0 == 0:
                            vtt(pl[:, 16:32], prev[:, 16:32], C["rc"][:, 16 * j:16 * j + 16], MUL)
                            h_ = 16
                        vts(pl[:, 16 + h_:16 + nr], prev[:, 16 + h_:16 + nr], 1.0 / d, None, MUL)
                        tp = vtt(up[:, 16:16 + nr], pl[:, 16:16 + nr], up[:, 16:16 + nr], SUB)
                        i, fr = take("hi")
                        m = mm(bank[i][:, 0:nr], wpl[:, 128 * j:128 * j + 128], up[:, 16:16 + nr], True, True, fr,
                               tp, t_wpl, mark=True)
                        bfree[i] = t_pool = act(mx[:, 4 + j, :], bank[i][:, 0:nr], ACT.Copy, m,
                                                scale=W["pscale"][:, j:j + 1])
                        yield True
                    wfree[wi] = P.last()
                for hf in range(2):
                    wi, w, tw = weights(A["wv2"][hf], 2048)
                    for t in range(nt):
                        i, fr = take()
                        for k in range(8):
                            m = mm(bank[i][:, 0:256], hT[:, k, 128 * t:128 * t + 128], w[:, 256 * k:256 * k + 256],
                                   k == 0, k == 7, fr, tw, tu, mark=(k == 7))
                        bfree[i] = t_v = act(vt[:, t0 + t, 256 * hf:256 * hf + 256], bank[i][:, 0:256], ACT.Copy, m, f)
                        yield True
                    wfree[wi] = P.last()
                i, fr = take()
                for t in range(nt):
                    for k in range(8):
                        m = mm(bank[i][:, 8 * t:8 * t + 8], hT[:, k, 128 * t:128 * t + 128], wsm[:, 8 * k:8 * k + 8],
                               k == 0, k == 7, fr, t_wsm, tu, mark=(k == 7))
                x3 = xx[:].rearrange("p (t h) -> p t h", t=nt)
                vtt(x3, bank[i][:, 0:8 * nt].rearrange("p (t h) -> p t h", t=nt), bmid(W["bf"], nt), ADD, m)
                bfree[i] = vts(xx[:], xx[:], -1.0, None, MUL)
                t_lf = softplus(lf[:, t0:t1, :].rearrange("p t h -> p (t h)"), xx[:], [q_[:] for q_ in sp])
                i, fr = take()
                for t in range(t0, t1):
                    for jt in range(t + 1):
                        m = mm(bank[i][:, 8 * (t - t0):8 * (t - t0) + 8], ut if jt == t else ones, lf[:, jt, :],
                               jt == 0, jt == t, fr, t_lf, mark=(jt == t))
                bfree[i] = vts(cq[:].rearrange("p t h -> p (t h)"), bank[i][:, 0:8 * nt], -1.0, None, MUL, None, m)
                for h in range(8):
                    i, fr = take()
                    for kt in range(t0, t1):
                        for jt in range(kt + 1):
                            m = mm(bank[i][:, 128 * (kt - t0):128 * (kt - t0) + 128],
                                   lf[:, jt, h:h + 1].to_broadcast([128, 128]), ut if jt == kt else ones,
                                   jt == 0, jt == kt, fr, mark=(jt == kt))
                    bfree[i] = t_cb = act(cb[:, h, q0:q0 + nr], bank[i][:, 0:nr], ACT.Copy, m, f)
                    yield True
                units = [(t, h) for t in range(t0, t1) for h in range(8)]
                held = {}

                def front(t, h, b):
                    kn = 128 * (t + 1)
                    i, fr = take("lo")
                    hp = 64 * (h % 2)
                    ps = bank[i]
                    mm(ps[:, 0:kn], qT[hp:hp + 64, h // 2, 128 * (t - t0):128 * (t - t0) + 128],
                       kT[hp:hp + 64, h // 2, 0:kn], True, False, fr, t_qk)
                    m = mm(ps[:, kn - 128:kn], ident, neg, False, True, mark=True)
                    V.cost += 0.07 + kn / 960.0
                    bfree[i] = V(lambda e: e.tensor_tensor_reduce(lg[b][:, 0:kn], ps[:, 0:kn], cb[:, h, 0:kn], 1.0,
                                                                  NEG, ADD, ALU.max, mxx[:, b:b + 1]),
                                 m, t_cb, held.get(("lg", b)))
                    vtt(mxx[:, 2 + b:3 + b], mxx[:, b:b + 1], cq[:, t - t0, h:h + 1], ADD)
                    tb = vtt(mxx[:, 4 + b:5 + b], cq[:, t - t0, h:h + 1], mxx[:, 2 + b:3 + b], SUB)
                    held[("e", b)] = act(lg[b][:, 0:kn], lg[b][:, 0:kn], ACT.Exp, tb, bias=mxx[:, 4 + b:5 + b],
                                         accum_out=den[:, h:h + 1] if t % 2 == 0 else mxx[:, 8 + h:9 + h])

                def turn_exp(t, h, b):
                    kn = 128 * (t + 1)
                    i, fr = take("hi")
                    if i in (4, 5):
                        i, fr = take("hi")
                        if i in (4, 5):
                            i, fr = take("hi")
                    for kt in range(t + 1):
                        m = tr(bank[i][:, 128 * kt:128 * kt + 128], lg[b][:, 128 * kt:128 * kt + 128], ident, fr,
                               held[("e", b)], mark=(kt == t))
                    held[("lg", b)] = m
                    bfree[i] = held[("t", b)] = act(pT[b][:, 0:kn], bank[i][:, 0:kn], ACT.Copy, m,
                                                    held.get(("pT", b)))
                    held[("den", t)] = held[("e", b)]

                def values(t, h, b):
                    tp = held[("t", b)]
                    io = 4 + t % 2
                    for kt in range(t + 1):
                        m = mm(bank[io][:, 64 * h:64 * h + 64], pT[b][:, 128 * kt:128 * kt + 128],
                               vt[:, kt, 64 * h:64 * h + 64], kt == 0, kt == t, tp, t_v, bfree[io], mark=(kt == t))
                    held[("pT", b)] = m
                    if h == 7:
                        dn = den[:] if t % 2 == 0 else mxx[:, 8:16]
                        recip(dn, dn, held[("den", t)])
                        ta = vtt(ao[:].rearrange("p (h e) -> p h e", h=8),
                                 bank[io][:].rearrange("p (h e) -> p h e", h=8), b3(dn, 64), MUL, m, held.get("ao"))
                        bfree[io] = ta
                        i, fr = take("lo")
                        for k in range(4):
                            m = tr(bank[i][:, 128 * k:128 * k + 128], ao[:, 128 * k:128 * k + 128], ident, fr, ta,
                                   mark=(k == 3))
                        held["ao"] = m
                        bfree[i] = got["t_at"] = act(mx[:, 0:4, 128 * (t - t0):128 * (t - t0) + 128],
                                                     bank[i][:].rearrange("p (k e) -> p k e", k=4), ACT.Copy, m)

                for u_ in range(len(units) + 2):
                    for lag, part in enumerate((front, turn_exp, values)):
                        if 0 <= u_ - lag < len(units):
                            part(*units[u_ - lag], (u_ - lag) % 2)
                            yield True
                for hf in range(4):
                    wi, w, tw = weights(A["wout2"][hf], 2048)
                    for t in range(nt):
                        i, fr = take()
                        for k in range(8):
                            m = mm(bank[i][:, 0:256], mx[:, k, 128 * t:128 * t + 128], w[:, 256 * k:256 * k + 256],
                                   k == 0, k == 7, fr, tw, got["t_at"], t_pool, mark=(k == 7))
                        hv = h2[:, t0 + t, 256 * hf:256 * hf + 256]
                        bfree[i] = th = vtt(hv, hv, bank[i][:, 0:256], ADD, m)
                        yield True
                    wfree[wi] = P.last()
        def feed(t0, t1, ol):
            pace[0] = 1.0
            nt = t1 - t0
            nr = 128 * nt
            f = fence()
            with ExitStack() as pa:
                ab = lambda nm, s, d=F32: sbx(pa, f"{nm}_{t0}", s, d)
                hT = ab("hT2", [128, 8, nr])
                fT = ab("fT", [128, 22, nr])
                flat = hT[:].rearrange("p k n -> p (k n)")
                ob = [flat[:, 1024 * b:1024 * b + 1024] for b in range(min(nt, 2))]
                yield from turned(hT, W["n2"], t0, t1, sm[:, 40:40 + nt], f)
                tu = got["turned"]
                for j in range(22):
                    wi, w, tw = weights(A["wgu"][j], 2048)
                    ps = []
                    for q_ in range(2):
                        i, fr = take(("lo", "hi")[q_])
                        for k in range(8):
                            m = mm(bank[i][:, 0:nr], w[:, q_ * 1024 + k * 128:q_ * 1024 + k * 128 + 128], hT[:, k, :],
                                   k == 0, k == 7, fr, tw, tu, mark=(k == 7))
                        ps.append((i, m))
                        yield True
                    wfree[wi] = P.last()
                    i, m = ps[0]
                    bfree[i] = ta = act(fT[:, j, :], bank[i][:, 0:nr], ACT.Silu, m, f)
                    i, m = ps[1]
                    bfree[i] = t_f = vtt(fT[:, j, :], fT[:, j, :], bank[i][:, 0:nr], MUL, m, ta, f)
                    yield True
                for hf in range(2):
                    bs = list(range(nt)) if hf == 0 else list(range(4, 4 + nt))
                    for k0, kn in ((0, 6), (6, 6), (12, 6), (18, 4)):
                        wi, w, tw = weights(A["wdn"][hf, :, 512 * k0:512 * (k0 + kn)], 512 * kn)
                        for k in range(k0, k0 + kn):
                            for t in range(nt):
                                m = mm(bank[bs[t]][:], fT[:, k, 128 * t:128 * t + 128],
                                       w[:, 512 * (k - k0):512 * (k - k0) + 512], k == 0, k == 21, bfree[bs[t]], tw,
                                       t_f, mark=(t == nt - 1))
                            yield True
                        wfree[wi] = P.last()
                    for t in range(nt):
                        hv = h2[:, t0 + t, 512 * hf:512 * hf + 512]
                        bfree[bs[t]] = th = vtt(hv, hv, bank[bs[t]][:], ADD, m)
                wi, w, tw = weights(A["fing"], 1024)
                for t in range(nt):
                    tt = act(junk[:], h2[:, t0 + t, :], ACT.Square, th, V.last(), accum_out=sm[:, t:t + 1])
                rsqrt(sm[:, 8:8 + nt], sm[:, 0:nt], (sm[:, 16:16 + nt], sm[:, 24:24 + nt]), 1.0 / 1024, tt)
                for t in range(nt):
                    tk = stt(ob[t % 2], h2[:, t0 + t, :], sm[:, 8 + t:9 + t], w[:, 0:1024], MUL, MUL, tw,
                             got.get(("ob", t % 2)))
                    got[("ob", t % 2)] = store(ol[t % 2], out[128 * (t0 + t):128 * (t0 + t) + 128, :], ob[t % 2], tk)
                wfree[wi] = V.last()
                yield True
                S.waits([got.get(("ob", b)) for b in range(2)])
                got["out"] = act(junk[:, 0:1], sm[:, 0:1], ACT.Copy, V.last(), P.last())

        done = set()
        pace = [1.0]

        def main():
            for t0, t1 in ASPLIT:
                yield from mixer(t0, t1)
                pace[0] = CW[t0 > 0]
                yield from choose(t0, t1)
                pace[0] = 1.0
            with ExitStack() as pk:
                bk = lambda nm, s: sbx(pk, nm, s)
                kv = (bk("kT", [128, 4, T]), bk("vt", [128, NT, 512]), bk("cb", [128, 8, T]), bk("lf", [128, NT, 8]),
                      bk("uh", [128, 4, 16]))
                ol = [lane(f"ol{i}") for i in range(2)]
                for what, t0, t1 in BSPLIT:
                    if what == "attend":
                        yield ("h3", t1 - 1)
                        yield from attend(t0, t1, kv)
                    else:
                        yield from feed(t0, t1, ol)

        t_rowa = load("l_rowa", rowa[:], A["lnffn"])
        t_rowb = load("l_rowb", rowb[:], A["lnfin"])
        t_wpl = load("l_wpl", wpl[:], A["wpool"])
        t_wsm = load("l_wsm", wsm[:], A["wf2"])
        t_x += [load(f"l_x{t}", h2[:, t, :], A["x"][128 * t:128 * t + 128, :]) for t in range(2, NT)]

        clock, gens, need = [0.0, 0.0], [main(), experts()], [None, None]
        while any(g is not None for g in gens):
            can = [i for i in range(2) if gens[i] is not None and (need[i] is None or need[i] in done)]
            i = min(can, key=lambda j: clock[j])
            if need[i] is not None:
                clock[i] = max(clock[i], clock[1 - i]) if gens[1 - i] is not None else clock[i]
                need[i] = None
            p, v = P.cost, V.cost
            V.stream = S.stream = ("main", "experts")[i]
            r = next(gens[i], None)
            if r is None:
                gens[i] = None
            elif isinstance(r, tuple):
                need[i] = r
            elif i == 0:
                clock[0] += pace[0] * max(P.cost - p, VW * (V.cost - v))
            else:
                clock[1] += r
        S.waits([got.get(("ob", b)) for b in range(2)])

        block = ctx.enter_context(nc.Block())
        block.sync(lambda e: D.emit(e))
        block.gpsimd(lambda e: Gp.emit(e))
        block.vector(lambda e: V.emit(e))
        block.scalar(lambda e: S.emit(e))
        block.tensor(lambda e: P.emit(e))


def laid_out(i):
    c = np.ascontiguousarray
    f = {k: np.asarray(v) for k, v in i.items()}
    w = f["w_in"][0].reshape(8, 128, 11296)

    def tiles(m, cols, kt):
        return m[:, :, cols].transpose(1, 0, 2).reshape(128, -1)

    def rows(v):
        return np.broadcast_to(v.reshape(1, -1), (128, v.size))

    def fm(v, n):
        return v.reshape(n, 128).T

    r = np.arange
    o = {}
    o["x"] = c(f["x"][0])
    o["meta"] = c(f["meta_tokens"])
    o["wdt"] = c(tiles(w, r(6144, 6176), 8))
    o["wg"] = c(np.stack([np.stack([
        tiles(w, np.concatenate([2048 + 256 * g + r(256), 4096 + 128 * g + r(128)]), 8),
        tiles(w, np.concatenate([5120 + 128 * g + r(128), 256 * g + r(256)]), 8)]) for g in range(8)]))
    o["wsc"] = c(np.stack([tiles(w, np.concatenate([6176 + 128 * j + r(128), 7200 + 128 * j + r(128),
                                                    8224 + 128 * j + r(128)]), 8) for j in range(8)]))
    wo_ = f["ssd_w_out"][0].reshape(16, 128, 1024)
    so_ = f["sc_w_out"][0].reshape(8, 128, 1024)
    o["wgate"] = c(np.stack([np.concatenate([
        tiles(w, 9248 + 128 * j + r(128), 8), tiles(w, 10272 + 128 * j + r(128), 8)], 1) for j in range(8)]))
    o["wso"] = c(np.stack([np.concatenate([
        tiles(wo_, 128 * j + r(128), 16), tiles(so_, 128 * j + r(128), 8)], 1) for j in range(8)]))
    w2 = f["w_o"][0].reshape(8, 128, 1024)
    o["wo"] = c(np.stack([tiles(w2, 256 * j + r(256), 8) for j in range(4)]))
    wq = f["peer_w_q"][0].reshape(8, 128, 2048)
    keys = f["peer_sub_keys"][0].reshape(16, 128, 128).transpose(2, 0, 1)
    o["wq"] = c(np.stack([np.concatenate([tiles(wq, 256 * a + r(128), 8), tiles(wq, 256 * a + 128 + r(128), 8),
                                          keys[:, 2 * a], keys[:, 2 * a + 1]], 1) for a in range(8)]))
    o["pu"] = c(f["peer_u"][0])
    o["pv"] = c(f["peer_v"][0])
    o["lnffn"] = c(rows(f["ln_ffn"][0]))
    o["lnfin"] = c(rows(f["ln_final"]))
    o["fing"] = c(rows(f["final_g_2"]))
    wi2 = f["w_in_2"][0]
    wi2 = wi2.reshape(8, 128, 2056)
    o["wqku"] = c(np.stack([np.concatenate([tiles(wi2, b + 128 * q + r(128), 8) for q in range(2)], 1)
                            for b in (0, 256, 512, 768, 1544, 1800)]))
    o["wv2"] = c(np.stack([tiles(wi2, 1024 + 256 * j + r(256), 8) for j in range(2)]))
    o["wf2"] = c(tiles(wi2, 1536 + r(8), 8))
    o["wpool"] = c(f["w_pool_2"][0].transpose(1, 0, 2).reshape(128, 512))
    wo2 = f["w_out_2"][0].reshape(8, 128, 1024)
    o["wout2"] = c(np.stack([tiles(wo2, 256 * j + r(256), 8) for j in range(4)]))
    wg, wu = f["w_gate_2"][0].reshape(8, 128, 2816), f["w_up_2"][0].reshape(8, 128, 2816)
    o["wgu"] = c(np.stack([np.concatenate([tiles(m, 128 * j + r(128), 8) for m in (wg, wu)], 1)
                           for j in range(22)]))
    wd = f["w_down_2"][0].reshape(22, 128, 1024)
    o["wdn"] = c(np.stack([tiles(wd, 512 * j + r(512), 22) for j in range(2)]))
    cw, cb = f["ssd_conv_w"][0], f["ssd_conv_b"][0]
    idx = [a + r(128) for g in range(8) for a in (256 * g, 256 * g + 128, 2048 + 128 * g, 3072 + 128 * g)]
    v = {"lnmix": fm(f["ln_mix"][0], 8), "convw": np.concatenate([cw[q] for q in idx], 1),
         "convb": np.stack([cb[q] for q in idx], 1), "dskip": fm(np.repeat(f["ssd_d"][0], 64), 16),
         "normg": fm(f["ssd_norm"][0], 16),
         "scw": f["sc_conv_w"][0].reshape(8, 128, 3).transpose(1, 0, 2).reshape(128, 24),
         "dtb": rows(f["ssd_dt_bias"][0]), "alog": rows(f["ssd_a_log"][0]), "n1": fm(f["norm1_g_2"][0], 8),
         "n2": fm(f["norm2_g_2"][0], 8), "bf": rows(f["b_forget_2"][0]), "pscale": fm(f["pool_scale_2"][0], 4),
         "lnffn": fm(f["ln_ffn"][0], 8)}
    o["vec"] = c(np.concatenate([v[k] for k in VEC], 1))
    p, q = np.meshgrid(r(128), r(128), indexing="ij")
    one_ = np.float32(1)
    rc = np.concatenate([1.0 / np.minimum(r(16) + 1, 2 << s) for s in range(4)])
    o["con"] = c(np.concatenate([(p == q) * one_, (p <= q) * one_, (p > q) * one_, (p < q) * np.float32(-1e30),
                                 np.ones((128, 128)), np.broadcast_to(r(16)[None], (128, 16)),
                                 np.broadcast_to(rc[None], (128, 64))], 1).astype(np.float32))
    return o


def kernel(**inputs):
    import concourse.bacc as bacc
    from concourse.bass_utils import run_bass_kernel_spmd

    nc = bacc.Bacc("TRN2", target_bir_lowering=False, num_devices=1)
    arrays = laid_out(inputs)
    A = {k: nc.dram_tensor("in_" + k, a.shape, F32, kind="ExternalInput").ap() for k, a in arrays.items()}
    out = nc.dram_tensor("out_0", (T, 1024), F32, kind="ExternalOutput").ap()
    build(nc, A, out)
    r = run_bass_kernel_spmd(nc, [{"in_" + k: a for k, a in arrays.items()}], core_ids=[0])
    return r.results[0]["out_0"].reshape(1, T, 1024)
```
